# Optimizing a Trainium2 kernel written in Bass

```python
import math
import jax, jax.numpy as jnp
from jax import lax
import numpy as np

D_MODEL = 1024
BATCH = 1
SEQ = 1024
DEPTH = 1

CTX_LEN = 256
GRID_W = 64
DN_HEAD_DIM = 128
DN_HEADS = D_MODEL // DN_HEAD_DIM
DN_DIM = DN_HEADS * DN_HEAD_DIM
SHORT_CONV = 5
CHUNK = 64
HEAD_DIM = 128
ATTN_HEADS = D_MODEL // HEAD_DIM
ATTN_KV_HEADS = ATTN_HEADS // 4
ATTN_GROUPS = ATTN_HEADS // ATTN_KV_HEADS
ATTN_DIM = ATTN_HEADS * HEAD_DIM
KV_DIM = ATTN_KV_HEADS * HEAD_DIM
WINDOW = 128
ATTN_BLOCK = 128
ROPE_BASE = 10000.0
ROPE_FREQS = HEAD_DIM // 4
D_FF = ((8 * D_MODEL // 3 + 127) // 128) * 128
FFN_CONV = 3
RMS_EPS = 1e-6
IN_SIZES = (3 * DN_DIM, DN_DIM, 2 * DN_HEADS, 2 * DN_HEADS, ATTN_DIM, KV_DIM, KV_DIM, 2 * D_MODEL)
IN_DIM = 4 * DN_DIM + 4 * DN_HEADS + ATTN_DIM + 2 * KV_DIM + 2 * D_MODEL

kernel_name = 'hybrid_deltanet_swa_dit_layer'

def rms_norm(x, w):
    xf = x.astype(jnp.float32)
    y = xf * lax.rsqrt(jnp.mean(xf * xf, axis=-1, keepdims=True) + RMS_EPS)
    return y.astype(x.dtype) * w

def l2_normalize(x):
    return x * lax.rsqrt(jnp.sum(x * x, axis=-1, keepdims=True) + RMS_EPS)

def modulate(h, shift, scale):
    return h * (1.0 + scale) + shift

def dwconv_centred(x, w):
    width = w.shape[0]
    r = width // 2
    length = x.shape[1]
    xp = jnp.pad(x, ((0, 0), (r, r), (0, 0)))
    out = xp[:, :length] * w[0]
    for j in range(1, width):
        out = out + xp[:, j:j + length] * w[j]
    return out

def split_in(p):
    cuts = np.cumsum(IN_SIZES)[:-1].tolist()
    return jnp.split(p, cuts, axis=-1)

def rope_tables_2d(rows, dtype):
    row = jnp.broadcast_to(jnp.arange(rows, dtype=jnp.float32)[:, None], (rows, GRID_W)).reshape(-1)
    col = jnp.broadcast_to(jnp.arange(GRID_W, dtype=jnp.float32)[None, :], (rows, GRID_W)).reshape(-1)
    inv_freq = ROPE_BASE ** (-jnp.arange(ROPE_FREQS, dtype=jnp.float32) / ROPE_FREQS)
    ang_r = row[:, None] * inv_freq
    ang_c = col[:, None] * inv_freq
    return (jnp.cos(ang_r).astype(dtype), jnp.sin(ang_r).astype(dtype),
            jnp.cos(ang_c).astype(dtype), jnp.sin(ang_c).astype(dtype))

def rope_1d(x, cos, sin):
    x1, x2 = jnp.split(x, 2, axis=-1)
    cos = cos[None, :, None, :]
    sin = sin[None, :, None, :]
    return jnp.concatenate([x1 * cos - x2 * sin, x2 * cos + x1 * sin], axis=-1)

def rope_2d(x, tables):
    cos_r, sin_r, cos_c, sin_c = tables
    half = HEAD_DIM // 2
    return jnp.concatenate([rope_1d(x[..., :half], cos_r, sin_r),
                            rope_1d(x[..., half:], cos_c, sin_c)], axis=-1)

def dn_prepare(qkv, b, a, conv_w, a_log, dt_bias):
    bsz, length = qkv.shape[:2]
    qkv = jax.nn.silu(dwconv_centred(qkv, conv_w)).astype(jnp.float32)
    q, k, v = jnp.split(qkv, 3, axis=-1)
    q = l2_normalize(q.reshape(bsz, length, DN_HEADS, DN_HEAD_DIM)) * (DN_HEAD_DIM ** -0.5)
    k = l2_normalize(k.reshape(bsz, length, DN_HEADS, DN_HEAD_DIM))
    v = v.reshape(bsz, length, DN_HEADS, DN_HEAD_DIM)
    beta = jax.nn.sigmoid(b.astype(jnp.float32)).reshape(bsz, length, 2, DN_HEADS)
    a = a.astype(jnp.float32).reshape(bsz, length, 2, DN_HEADS)
    g = -jnp.exp(a_log.astype(jnp.float32)) * jax.nn.softplus(a + dt_bias.astype(jnp.float32))
    return q, k, v, g, beta

def gated_delta_chunked(q, k, v, g, beta, s0):
    bsz, length, heads, _ = q.shape
    dv = v.shape[-1]
    n = length // CHUNK

    def to_chunks(t):
        t = t.reshape((bsz, n, CHUNK, heads) + t.shape[3:])
        return jnp.moveaxis(t, (1, 3), (0, 2))

    qc, kc, vc, bc = to_chunks(q), to_chunks(k), to_chunks(v), to_chunks(beta)
    gc = jnp.cumsum(to_chunks(g), axis=-1)
    idx = jnp.arange(CHUNK)
    incl = idx[:, None] >= idx[None, :]
    strict = idx[:, None] > idx[None, :]
    diff = gc[..., :, None] - gc[..., None, :]
    decay = jnp.where(incl, jnp.exp(jnp.where(incl, diff, 0.0)), 0.0)
    kk = jnp.einsum('nbhid,nbhjd->nbhij', kc, kc)
    a_mat = jnp.where(strict, bc[..., :, None] * kk * decay, 0.0)
    rhs = jnp.concatenate([vc * bc[..., None], kc * (bc * jnp.exp(gc))[..., None]], axis=-1)
    sol = lax.linalg.triangular_solve(a_mat, rhs, left_side=True, lower=True, unit_diagonal=True)
    u, w = sol[..., :dv], sol[..., dv:]
    qk = jnp.einsum('nbhid,nbhjd->nbhij', qc, kc) * decay
    qg = qc * jnp.exp(gc)[..., None]
    kd = kc * jnp.exp(gc[..., -1:] - gc)[..., None]
    g_last = jnp.exp(gc[..., -1])

    def step(s, xs):
        u_i, w_i, qg_i, qk_i, kd_i, gl_i = xs
        v_new = u_i - jnp.einsum('bhcd,bhde->bhce', w_i, s)
        o_i = jnp.einsum('bhcd,bhde->bhce', qg_i, s) + jnp.einsum('bhij,bhje->bhie', qk_i, v_new)
        s = s * gl_i[..., None, None] + jnp.einsum('bhcd,bhce->bhde', kd_i, v_new)
        return s, o_i

    s_fin, o = lax.scan(step, s0, (u, w, qg, qk, kd, g_last))
    o = jnp.moveaxis(o, (0, 2), (1, 3)).reshape(bsz, length, heads, dv)
    return o, s_fin

def bidirectional_delta(lat, ctx_side):
    qx, kx, vx, gx, bx = lat
    qc, kc, vc, gc, bc = ctx_side
    s0 = jnp.zeros((qc.shape[0], DN_HEADS, DN_HEAD_DIM, DN_HEAD_DIM), jnp.float32)
    rev = lambda t: jnp.flip(t, axis=1)
    oc_f, sc_f = gated_delta_chunked(qc, kc, vc, gc[:, :, 0], bc[:, :, 0], s0)
    ox_f, _ = gated_delta_chunked(qx, kx, vx, gx[:, :, 0], bx[:, :, 0], sc_f)
    oc_b, sc_b = gated_delta_chunked(rev(qc), rev(kc), rev(vc), rev(gc[:, :, 1]), rev(bc[:, :, 1]), s0)
    ox_b, _ = gated_delta_chunked(rev(qx), rev(kx), rev(vx), rev(gx[:, :, 1]), rev(bx[:, :, 1]), sc_b)
    return ox_f + rev(ox_b), oc_f + rev(oc_b)

def gated_head_norm(o, gate, w):
    bsz, length = o.shape[:2]
    y = rms_norm(o, w) * jax.nn.silu(gate.reshape(bsz, length, DN_HEADS, DN_HEAD_DIM).astype(jnp.float32))
    return y.reshape(bsz, length, DN_DIM).astype(gate.dtype)

def attn_heads(q, k, v, q_norm, k_norm):
    bsz, length = q.shape[:2]
    q = rms_norm(q.reshape(bsz, length, ATTN_HEADS, HEAD_DIM), q_norm)
    k = rms_norm(k.reshape(bsz, length, ATTN_KV_HEADS, HEAD_DIM), k_norm)
    v = v.reshape(bsz, length, ATTN_KV_HEADS, HEAD_DIM)
    return q, k, v

def window_attention_latent(q, k, v, k_ctx, v_ctx, sink):
    bsz, length = q.shape[:2]
    n_ctx = k_ctx.shape[1]
    nb = length // ATTN_BLOCK
    band = 3 * ATTN_BLOCK
    scale = HEAD_DIM ** -0.5
    pad = ((0, 0), (ATTN_BLOCK, ATTN_BLOCK), (0, 0), (0, 0))
    kp = jnp.pad(k, pad)
    vp = jnp.pad(v, pad)
    qb = jnp.moveaxis(q.reshape(bsz, nb, ATTN_BLOCK, ATTN_KV_HEADS, ATTN_GROUPS, HEAD_DIM), 1, 0)
    sink_l = jnp.broadcast_to(sink.astype(jnp.float32).reshape(1, ATTN_KV_HEADS, ATTN_GROUPS, 1, 1),
                              (bsz, ATTN_KV_HEADS, ATTN_GROUPS, ATTN_BLOCK, 1))

    def block(args):
        i, q_i = args
        start = i * ATTN_BLOCK
        k_i = lax.dynamic_slice_in_dim(kp, start, band, axis=1)
        v_i = lax.dynamic_slice_in_dim(vp, start, band, axis=1)
        qpos = start + jnp.arange(ATTN_BLOCK)
        kpos = start - ATTN_BLOCK + jnp.arange(band)
        ok = (jnp.abs(qpos[:, None] - kpos[None, :]) <= WINDOW) & (kpos[None, :] >= 0) & (kpos[None, :] < length)
        s_win = jnp.einsum('bqkgd,bskd->bkgqs', q_i, k_i).astype(jnp.float32) * scale
        s_win = jnp.where(ok, s_win, -jnp.inf)
        s_ctx = jnp.einsum('bqkgd,bskd->bkgqs', q_i, k_ctx).astype(jnp.float32) * scale
        p = jax.nn.softmax(jnp.concatenate([s_win, s_ctx, sink_l], axis=-1), axis=-1).astype(v.dtype)
        return (jnp.einsum('bkgqs,bskd->bqkgd', p[..., :band], v_i)
                + jnp.einsum('bkgqs,bskd->bqkgd', p[..., band:band + n_ctx], v_ctx))

    o = lax.map(block, (jnp.arange(nb), qb))
    return jnp.moveaxis(o, 0, 1).reshape(bsz, length, ATTN_DIM)

def context_attention(q, k, v, sink):
    bsz, n_ctx = q.shape[:2]
    qg = q.reshape(bsz, n_ctx, ATTN_KV_HEADS, ATTN_GROUPS, HEAD_DIM)
    s = jnp.einsum('bqkgd,bskd->bkgqs', qg, k).astype(jnp.float32) * (HEAD_DIM ** -0.5)
    sink_c = jnp.broadcast_to(sink.astype(jnp.float32).reshape(1, ATTN_KV_HEADS, ATTN_GROUPS, 1, 1),
                              (bsz, ATTN_KV_HEADS, ATTN_GROUPS, n_ctx, 1))
    p = jax.nn.softmax(jnp.concatenate([s, sink_c], axis=-1), axis=-1).astype(v.dtype)
    o = jnp.einsum('bkgqs,bskd->bqkgd', p[..., :n_ctx], v)
    return o.reshape(bsz, n_ctx, ATTN_DIM)

def merge_branches(y_dn, y_at, gates, w_branch_dn, w_branch_attn, w_out):
    g_dn, g_at = jnp.split(gates, 2, axis=-1)
    merged = jax.nn.sigmoid(g_dn) * (y_dn @ w_branch_dn) + jax.nn.sigmoid(g_at) * (y_at @ w_branch_attn)
    return merged @ w_out

def conv_ffn(h, up, conv_w, conv_b, down):
    u = dwconv_centred(h @ up, conv_w) + conv_b
    u_gate, u_val = jnp.split(u, 2, axis=-1)
    return (jax.nn.silu(u_gate) * u_val) @ down

def hybrid_layer(x, ctx, c, c_ctx, rope, w_ada, b_ada, norm_mix, norm_ffn, w_in, dn_conv, dn_a_log,
                 dn_dt_bias, dn_norm, q_norm, k_norm, attn_sink, w_branch_dn, w_branch_attn, w_out,
                 ffn_up, ffn_conv, ffn_conv_b, ffn_down, update_ctx):
    mod_x = (jax.nn.silu(c) @ w_ada + b_ada)[:, None, :]
    mod_c = (jax.nn.silu(c_ctx) @ w_ada + b_ada)[None, None, :]
    sh_a_x, sc_a_x, g_a_x, sh_f_x, sc_f_x, g_f_x = jnp.split(mod_x, 6, axis=-1)
    sh_a_c, sc_a_c, g_a_c, sh_f_c, sc_f_c, g_f_c = jnp.split(mod_c, 6, axis=-1)

    p_x = modulate(rms_norm(x, norm_mix), sh_a_x, sc_a_x) @ w_in
    p_c = modulate(rms_norm(ctx, norm_mix), sh_a_c, sc_a_c) @ w_in
    qkv_dn_x, gt_dn_x, b_dn_x, a_dn_x, q_at_x, k_at_x, v_at_x, mg_x = split_in(p_x)
    qkv_dn_c, gt_dn_c, b_dn_c, a_dn_c, q_at_c, k_at_c, v_at_c, mg_c = split_in(p_c)

    dn_x = dn_prepare(qkv_dn_x, b_dn_x, a_dn_x, dn_conv, dn_a_log, dn_dt_bias)
    dn_c = dn_prepare(qkv_dn_c, b_dn_c, a_dn_c, dn_conv, dn_a_log, dn_dt_bias)
    o_dn_x, o_dn_c = bidirectional_delta(dn_x, dn_c)
    y_dn_x = gated_head_norm(o_dn_x, gt_dn_x, dn_norm)

    qx, kx, vx = attn_heads(q_at_x, k_at_x, v_at_x, q_norm, k_norm)
    qc, kc, vc = attn_heads(q_at_c, k_at_c, v_at_c, q_norm, k_norm)
    qx = rope_2d(qx, rope)
    kx = rope_2d(kx, rope)
    y_at_x = window_attention_latent(qx, kx, vx, kc, vc, attn_sink)

    x = x + g_a_x * merge_branches(y_dn_x, y_at_x, mg_x, w_branch_dn, w_branch_attn, w_out)
    x = x + g_f_x * conv_ffn(modulate(rms_norm(x, norm_ffn), sh_f_x, sc_f_x), ffn_up, ffn_conv, ffn_conv_b, ffn_down)

    if update_ctx:
        y_dn_c = gated_head_norm(o_dn_c, gt_dn_c, dn_norm)
        y_at_c = context_attention(qc, kc, vc, attn_sink)
        ctx = ctx + g_a_c * merge_branches(y_dn_c, y_at_c, mg_c, w_branch_dn, w_branch_attn, w_out)
        ctx = ctx + g_f_c * conv_ffn(modulate(rms_norm(ctx, norm_ffn), sh_f_c, sc_f_c), ffn_up, ffn_conv, ffn_conv_b, ffn_down)
    return x, ctx

def setup_inputs(seed: int = 0) -> dict:
    key = jax.random.key(seed)
    ks = jax.random.split(key, 24)

    def nrm(k, shape, s):
        return jax.random.normal(k, shape, jnp.float32) * s

    x = nrm(ks[0], (BATCH, SEQ, D_MODEL), 1.0)
    c = nrm(ks[1], (BATCH, D_MODEL), 1.0)
    ctx = nrm(ks[2], (BATCH, CTX_LEN, D_MODEL), 1.0)
    c_ctx = nrm(ks[3], (D_MODEL,), 1.0)
    w_ada = nrm(ks[4], (DEPTH, D_MODEL, 6 * D_MODEL), 0.5 * D_MODEL ** -0.5)
    b_ada = nrm(ks[5], (DEPTH, 6 * D_MODEL), 0.02)
    norm_mix = 1.0 + nrm(ks[6], (DEPTH, D_MODEL), 0.1)
    norm_ffn = 1.0 + nrm(ks[7], (DEPTH, D_MODEL), 0.1)
    w_in = nrm(ks[8], (DEPTH, D_MODEL, IN_DIM), D_MODEL ** -0.5)
    dn_conv = nrm(ks[9], (DEPTH, SHORT_CONV, 3 * DN_DIM), SHORT_CONV ** -0.5)
    dn_a_log = jnp.log(jax.random.uniform(ks[10], (DEPTH, 2, DN_HEADS), jnp.float32, minval=1.0, maxval=16.0))
    dt = jnp.exp(jax.random.uniform(ks[11], (DEPTH, 2, DN_HEADS), jnp.float32,
                                    minval=math.log(1e-3), maxval=math.log(1e-1)))
    dn_dt_bias = dt + jnp.log(-jnp.expm1(-dt))
    dn_norm = 1.0 + nrm(ks[12], (DEPTH, DN_HEAD_DIM), 0.1)
    q_norm = 1.0 + nrm(ks[13], (DEPTH, HEAD_DIM), 0.1)
    k_norm = 1.0 + nrm(ks[14], (DEPTH, HEAD_DIM), 0.1)
    attn_sink = nrm(ks[15], (DEPTH, ATTN_HEADS), 0.5)
    w_branch_dn = nrm(ks[16], (DEPTH, DN_DIM, D_MODEL), DN_DIM ** -0.5)
    w_branch_attn = nrm(ks[17], (DEPTH, ATTN_DIM, D_MODEL), ATTN_DIM ** -0.5)
    w_out = nrm(ks[18], (DEPTH, D_MODEL, D_MODEL), D_MODEL ** -0.5)
    ffn_up = nrm(ks[19], (DEPTH, D_MODEL, 2 * D_FF), D_MODEL ** -0.5)
    ffn_conv = nrm(ks[20], (DEPTH, FFN_CONV, 2 * D_FF), FFN_CONV ** -0.5)
    ffn_conv_b = nrm(ks[21], (DEPTH, 2 * D_FF), 0.02)
    ffn_down = nrm(ks[22], (DEPTH, D_FF, D_MODEL), D_FF ** -0.5)
    return {'x': x, 'c': c, 'ctx': ctx, 'c_ctx': c_ctx, 'w_ada': w_ada, 'b_ada': b_ada,
            'norm_mix': norm_mix, 'norm_ffn': norm_ffn, 'w_in': w_in, 'dn_conv': dn_conv,
            'dn_a_log': dn_a_log, 'dn_dt_bias': dn_dt_bias, 'dn_norm': dn_norm, 'q_norm': q_norm,
            'k_norm': k_norm, 'attn_sink': attn_sink, 'w_branch_dn': w_branch_dn,
            'w_branch_attn': w_branch_attn, 'w_out': w_out, 'ffn_up': ffn_up, 'ffn_conv': ffn_conv,
            'ffn_conv_b': ffn_conv_b, 'ffn_down': ffn_down}

def reference(x, c, ctx, c_ctx, w_ada, b_ada, norm_mix, norm_ffn, w_in, dn_conv, dn_a_log, dn_dt_bias,
              dn_norm, q_norm, k_norm, attn_sink, w_branch_dn, w_branch_attn, w_out, ffn_up, ffn_conv,
              ffn_conv_b, ffn_down):
    rows = x.shape[1] // GRID_W
    rope = rope_tables_2d(rows, x.dtype)
    for layer in range(DEPTH):
        x, ctx = hybrid_layer(x, ctx, c, c_ctx, rope, w_ada[layer], b_ada[layer], norm_mix[layer],
                              norm_ffn[layer], w_in[layer], dn_conv[layer], dn_a_log[layer],
                              dn_dt_bias[layer], dn_norm[layer], q_norm[layer], k_norm[layer],
                              attn_sink[layer], w_branch_dn[layer], w_branch_attn[layer], w_out[layer],
                              ffn_up[layer], ffn_conv[layer], ffn_conv_b[layer], ffn_down[layer],
                              update_ctx=layer + 1 < DEPTH)
    return x


_drawn_inputs = setup_inputs


def setup_inputs(seed=0):
    import zlib

    import numpy as np

    out = dict(_drawn_inputs(seed))
    spreads = {}
    factors = {'ctx': 5.039,
     'b_ada': 2.922,
     'norm_mix': 3.092,
     'dn_a_log': 2.791,
     'dn_norm': 5.227,
     'q_norm': 8.0,
     'k_norm': 8.0,
     'attn_sink': 8.0,
     'ffn_conv_b': 23.219,
     'norm_ffn': 4.495}
    for name, (base, spread) in spreads.items():
        noise = np.random.default_rng([zlib.crc32(name.encode()), seed]).standard_normal(out[name].shape)
        drawn = base * np.exp(spread * noise) if base else spread * noise
        out[name] = __import__('jax').numpy.asarray(drawn.astype(out[name].dtype))
    for name, factor in factors.items():
        out[name] = (out[name] * factor).astype(out[name].dtype)
    return out
```

```python
import math
from contextlib import ExitStack

import numpy as np
import concourse.bass as bass
from concourse import mybir

F32 = mybir.dt.float32
F32R = mybir.dt.float32r
BF16 = mybir.dt.bfloat16
F16 = mybir.dt.float16
ALU = mybir.AluOpType
ACT = mybir.ActivationFunctionType
AX = mybir.AxisListType

P = 128
D_MODEL = 1024
SEQ = 1024
CTX = 256
TOK = SEQ + CTX
KT = D_MODEL // P
HALF = 512
HEADS = 8
KV_HEADS = 2
GROUPS = HEADS // KV_HEADS
D_FF = 2816
FT = D_FF // P
TAPS = 5
FTAPS = 3
EPS = 1e-6
GRID_W = 64
CH = 128
XCH = SEQ // CH
NCH = TOK // CH
LEVELS = 7
NEG = -1.0e30
RANGES = [(0, HALF), (HALF, HALF), (SEQ, CTX)]

COL_Q, COL_K, COL_V, COL_GATE = 0, 1024, 2048, 3072
COL_BA = 4096
COL_AQ, COL_AK, COL_AV = 4128, 5152, 5408
COL_MG_DN, COL_MG_AT = 5664, 6688

V_C = 0
V_BADA = V_C + 2 * KT
V_NMIX = V_BADA + 48
V_NFFN = V_NMIX + KT
V_DNNORM = V_NFFN + KT
V_QKN = V_DNNORM + 1
V_CONVB = V_QKN + HEADS + KV_HEADS
V_CONVF = V_CONVB + 2 * FT
V_CONVD = V_CONVF + 2 * FT * FTAPS
V_SINK = V_CONVD + HEADS * 3 * TAPS
V_ALOG = V_SINK + HEADS
V_DT = V_ALOG + 2 * HEADS
NVEC = V_DT + 2 * HEADS

C_ID, C_ONE, C_ROT, C_LT, C_GT, C_LE, C_GE, C_NEGLT, C_NEGGT = range(9)
C_LEVEL = 9
C_FIRST_T = C_LEVEL + 2 * LEVELS
NCONST = C_FIRST_T + 2


def constants():
    r, c = np.arange(P)[:, None], np.arange(P)[None, :]
    rot = np.zeros((P, P), np.float32)
    for base in (0, 64):
        for d in range(32):
            rot[base + 32 + d, base + d] = -1.0
            rot[base + d, base + 32 + d] = 1.0
    mats = [r == c, r >= 0, rot, c < r, c > r, c <= r, c >= r, NEG * (c < r), NEG * (c > r)]
    for level in range(LEVELS):
        s = 1 << level
        m = (r // (2 * s) == c // (2 * s)) & ((r // s) % 2 == 1) & ((c // s) % 2 == 0)
        unit = 1.0 * (r == c) if level == 0 else 0.0
        mats += [unit - m, unit - m.T]
    mats += [mats[C_LEVEL + 1], mats[C_LEVEL]]
    mats = np.stack([np.broadcast_to(m, (P, P)) for m in mats], 1).astype(np.float32)
    inv_freq = (np.float32(10000.0) ** (-np.arange(32, dtype=np.float32) / np.float32(32))).astype(np.float32)
    t = np.arange(SEQ)
    ang_r = (t // GRID_W).astype(np.float32)[None, :] * inv_freq[:, None]
    ang_c = (t % GRID_W).astype(np.float32)[None, :] * inv_freq[:, None]
    ang = np.concatenate([ang_r, ang_r, ang_c, ang_c], 0)
    return mats, np.stack([np.cos(ang), np.sin(ang)], 1).astype(np.float32)


SLOT_T = 4


class Core:

    def __init__(self, nc, ctx):
        self.nc, self.ctx = nc, ctx
        self.sems = []

    def sb(self, name, shape, dt=F32, ctx=None):
        return (ctx or self.ctx).enter_context(self.nc.sbuf_tensor(name, shape, dt))

    def ps(self, name, shape, dt=F32, ctx=None):
        return (ctx or self.ctx).enter_context(self.nc.psum_tensor(name, shape, dt))

    def sem(self, name):
        self.sems.append(self.nc.alloc_semaphore(name))
        return self.sems[-1]

    def retire_semaphores(self):
        self.nc.clear_and_free_semaphores(self.sems)
        self.sems = []
        self.nc.all_engine_barrier()


class Count:

    def __init__(self, core, name, slack=16):
        self.sem, self.slack = core.sem(name), slack

    def open(self, eng):
        eng.sem_inc(self.sem, self.slack)

    def wait(self, eng, n):
        eng.wait_ge(self.sem, n + self.slack)


class Weights:

    HI, LO = 2, 4

    def __init__(self, core, st, tag, kt=KT, at=None):
        self.kt = kt

        def slot(name, n, dt):
            if at is None:
                return core.sb(name, [P, kt, P], dt, ctx=st)
            return core.nc.alloc_sbuf_tensor_at(name, [P, kt, P], dt, offset=at + n * kt * P * 4)

        def pair(name, n):
            if at is None:
                return core.sb(name, [P, 2, kt, P], F32R, ctx=st)
            return core.nc.alloc_sbuf_tensor_at(name, [P, 2, kt, P], F32R, offset=at + n * kt * P * 4)
        self.raw = [slot(f"{tag}_w_raw{j}", j, F32) for j in range(2)]
        self.hi2, self.lo2 = pair(f"{tag}_w_hi", self.HI), pair(f"{tag}_w_lo", self.LO)
        self.hi, self.lo = ([t[:, j, :, :] for j in range(2)] for t in (self.hi2, self.lo2))
        self.loaded = [core.sem(f"{tag}_w_loaded{j}") for j in range(2)]
        self.hi_made = core.sem(f"{tag}_w_hi_made")
        self.split = core.sem(f"{tag}_w_split")
        self.used = Count(core, f"{tag}_w_tiles_used")
        self.turns = core.sem(f"{tag}_w_turns")

    def load(self, sp, t, src, j, first=False):
        if not first:
            sp.wait_ge(self.split, t - 1)
        sp.dma_start(self.raw[j][:, :, :], src).then_inc(self.loaded[j], 16)

    def split_tile(self, pool, t, half, j, freed=True, by=None):
        pool.wait_ge(self.loaded[j], half * 16 + 16)
        if by is not None:
            by[0].wait(pool, by[1])
        elif freed:
            self.used.wait(pool, t - 1)
        pool.sem_inc(self.turns, 1)
        pool.tensor_copy(self.hi[j][:, :, :], self.raw[j][:, :, :]).then_inc(self.hi_made, 1)
        pool.wait_ge(self.hi_made, t + 1)
        pool.tensor_tensor(self.lo[j][:, :, :], self.raw[j][:, :, :], self.hi[j][:, :, :].bitcast(F32),
                           ALU.subtract).then_inc(self.split, 1)

    def product(self, pe, out, j, hi, lo, lo_tok, n, parts=None):
        for k in range(self.kt):
            if parts is not None:
                pe.wait_ge(parts, k + 1)
            xh, xl = hi[:, k, lo_tok:lo_tok + n], lo[:, k, lo_tok:lo_tok + n]
            pe.matmul(out, self.hi[j][:, k, :], xh, start=(k == 0), stop=False)
            pe.matmul(out, self.hi[j][:, k, :], xl, start=False, stop=False)
            mm = pe.matmul(out, self.lo[j][:, k, :], xh, start=False, stop=(k == self.kt - 1))
        return mm


def modulation_and_norm(core, d):
    nc, vec, mats = core.nc, core.vec, core.mats
    NLOAD = 2 * KT // SLOT_T
    with ExitStack() as st:
        x = core.sb("x_in", [P, KT, TOK], ctx=st)
        sq = core.sb("x_squares", [P, 2, TOK], ctx=st)
        rstd = core.sb("x_rstd", [P, TOK], ctx=st)
        xn = core.sb("x_normed", [P, 2, TOK], ctx=st)
        hf = core.sb("h_full", [P, 2, TOK], ctx=st)
        w_ada = [core.sb(f"w_ada{j}", [P, KT, SLOT_T * P], ctx=st) for j in range(2)]
        silu_c = core.silu_c
        ps_ss = core.ps("ps_sum_sq", [P, 3, HALF], ctx=st)
        ps_mod = core.ps("ps_mod", [P, 2 * KT, 2], ctx=st)
        consts_in = core.sem("consts_in")
        x_in = [core.sem(f"x_in{k}") for k in range(KT)]
        ada_in = [core.sem(f"ada_in{j}") for j in range(2)]
        silu_ready, ada_used, mod_done = core.sem("silu_ready"), core.sem("ada_used"), core.sem("mod_done")
        sq_ready, sq_used, ss_done = core.sem("sq_ready"), core.sem("sq_used"), core.sem("ss_done")
        std_ready, rstd_ready = core.sem("std_ready"), core.sem("rstd_ready")
        eps_ready, mod_ready, scale_ready = core.sem("eps_ready"), core.sem("mod_ready"), core.sem("scale_ready")
        xn_ready, hi_ready, hf_ready, lo_ready = (core.sem("xn_ready"), core.sem("h_hi_ready"),
                                                  core.sem("h_full_ready"), core.sem("h_lo_ready"))
        const_copies = core.sem("const_copies")
        def modulation(dve):
            dve.wait_ge(ada_used, NLOAD)
            b = vec[:, V_BADA:V_BADA + 2 * KT]
            for s in range(2):
                dve.tensor_tensor(core.mod[:, 0:2 * KT, s], ps_mod[:, :, s], b, ALU.add).then_inc(mod_ready, 1)
            dve.wait_ge(mod_ready, 2)
            for s in range(2):
                dve.scalar_tensor_tensor(out=core.scale_mix[:, :, s], in0=core.mod[:, KT:2 * KT, s], scalar=1.0,
                                         in1=vec[:, V_NMIX:V_NMIX + KT], op0=ALU.add,
                                         op1=ALU.mult).then_inc(scale_ready, 1)

        def low(dve, k):
            dve.wait_ge(hf_ready, 2 * (k + 1))
            dve.wait_ge(hi_ready, 2 * (k + 1))
            dve.tensor_tensor(core.h_lo[:, k, :], hf[:, k % 2, :], core.h_hi[:, k, :].bitcast(F32),
                              ALU.subtract).then_inc(lo_ready, 1)

        with nc.Block() as block:
            @block.sync
            def _(sp):
                sp.dma_start(vec[:, :], d["vec"]).then_inc(consts_in, 16)
                sp.dma_start(mats[:, :, :], d["mats"]).then_inc(consts_in, 16)
                for k in range(KT):
                    sp.dma_start(x[:, k, :], d["xT"][:, k, :]).then_inc(x_in[k], 16)
                for n in range(NLOAD):
                    if n >= 2:
                        sp.wait_ge(ada_used, n - 1)
                    sp.dma_start(w_ada[n % 2][:, :, :], d["w_ada"][:, n]).then_inc(ada_in[n % 2], 16)

            @block.tensor
            def _(pe):
                pe.wait_ge(consts_in, 32)
                for k in range(KT):
                    pe.wait_ge(sq_ready, k + 1)
                    for b, (t0, n) in enumerate(RANGES):
                        mm = pe.matmul(ps_ss[:, b, 0:n], mats[:, C_ONE, :], sq[:, k % 2, t0:t0 + n],
                                       start=(k == 0), stop=(k == KT - 1))
                    mm.then_inc(ss_done, 1)
                pe.wait_ge(silu_ready, 1)
                for n in range(NLOAD):
                    pe.wait_ge(ada_in[n % 2], 16 * (n // 2 + 1))
                    for m in range(SLOT_T):
                        for k in range(KT):
                            mm = pe.matmul(ps_mod[:, n * SLOT_T + m, :], w_ada[n % 2][:, k, m * P:(m + 1) * P],
                                           silu_c[:, k, :], start=(k == 0), stop=(k == KT - 1))
                    mm.then_inc(ada_used, 1)

            @block.scalar
            def _(act):
                act.wait_ge(consts_in, 32)
                act.activation(silu_c[:, :, :], vec[:, V_C:V_C + 2 * KT].rearrange("p (k s) -> p k s", s=2),
                               ACT.Silu).then_inc(silu_ready, 1)
                for k in range(KT):
                    act.wait_ge(x_in[k], 16)
                    if k >= 2:
                        act.wait_ge(ss_done, k - 1)
                    act.activation(sq[:, k % 2, :], x[:, k, :], ACT.Square).then_inc(sq_ready, 1)
                act.wait_ge(ss_done, KT)
                act.wait_ge(eps_ready, 1)
                for b, (t0, n) in enumerate(RANGES):
                    act.activation(rstd[:, t0:t0 + n], ps_ss[:, b, 0:n], ACT.Sqrt, scale=1.0 / D_MODEL,
                                   bias=core.eps[:, 0:1]).then_inc(std_ready, 1)
                act.activation(core.id_h[:, :], mats[:, C_ID, :], ACT.Copy).then_inc(const_copies, 1)
                act.activation(core.id_b[:, :], mats[:, C_ID, :], ACT.Copy).then_inc(const_copies, 1)
                act.activation(core.neg_b[:, :, :], mats[:, C_NEGLT:C_NEGLT + 2, :], ACT.Copy).then_inc(const_copies, 1)
                act.wait_ge(scale_ready, 2)
                for k in range(KT):
                    act.wait_ge(xn_ready, k + 1)
                    if k >= 2:
                        act.wait_ge(lo_ready, k - 1)
                    for s, (t0, n) in enumerate(((0, SEQ), (SEQ, CTX))):
                        sc, sh = core.scale_mix[:, k, s:s + 1], core.mod[:, k, s:s + 1]
                        act.activation(core.h_hi[:, k, t0:t0 + n], xn[:, k % 2, t0:t0 + n], ACT.Identity,
                                       bias=sh, scale=sc).then_inc(hi_ready, 1)
                        act.activation(hf[:, k % 2, t0:t0 + n], xn[:, k % 2, t0:t0 + n], ACT.Identity,
                                       bias=sh, scale=sc).then_inc(hf_ready, 1)

            @block.vector
            def _(dve):
                dve.memset(core.eps[:, 0:1], EPS).then_inc(eps_ready, 1)
                dve.memset(core.eps[:, 1:2], P * EPS).then_inc(eps_ready, 1)
                for b, (t0, n) in enumerate(RANGES):
                    dve.wait_ge(std_ready, b + 1)
                    dve.reciprocal(rstd[:, t0:t0 + n], rstd[:, t0:t0 + n]).then_inc(rstd_ready, 1)
                dve.wait_ge(rstd_ready, 3)
                dve.wait_ge(x_in[0], 16)
                for k in range(KT):
                    if k >= 2:
                        dve.wait_ge(hf_ready, 2 * (k - 1))
                        dve.wait_ge(hi_ready, 2 * (k - 1))
                    dve.wait_ge(x_in[k], 16)
                    dve.tensor_tensor(xn[:, k % 2, :], x[:, k, :], rstd[:, :], ALU.mult).then_inc(xn_ready, 1)
                    if k == 0:
                        modulation(dve)
                    if k >= 1:
                        low(dve, k - 1)
                low(dve, KT - 1)


def attention_projections(core, d, a):
    nc, vec, mats = core.nc, core.vec, core.mats
    NT = HEADS + KV_HEADS
    with ExitStack() as st:
        w = Weights(core, st, "aproj")
        rope = core.sb("rope_tables", [P, 2, SEQ], ctx=st)
        sq = core.sb("qk_squares", [P, SEQ], ctx=st)
        raw = core.sb("qk_raw", [P, SEQ], ctx=st)
        std = core.sb("qk_std", [P, SEQ], ctx=st)
        rs = core.sb("qk_rstd", [P, SEQ], ctx=st)
        qn = core.sb("qk_normed", [P, SEQ], ctx=st)
        by_cos = core.sb("qk_by_cos", [P, SEQ], ctx=st)
        w_ba = core.sb("w_ba", [P, KT, 32], ctx=st)
        w_ba_hi = core.sb("w_ba_hi", [P, KT, 32], F32R, ctx=st)
        w_ba_lo = core.sb("w_ba_lo", [P, KT, 32], F32R, ctx=st)
        ps_main = [core.ps(f"ps_qk{j}", [P, SEQ], ctx=st) for j in range(2)]
        ps_ss = core.ps("ps_qk_ss", [P, SEQ], ctx=st)
        ps_rot = core.ps("ps_rot", [P, SEQ], ctx=st)
        ss_done, rot_done = Count(core, "qk_ss_done"), Count(core, "rot_done")
        sq_ready, raw_ready, std_ready = Count(core, "qk_sq"), Count(core, "qk_raw_ready"), Count(core, "qk_std_ready")
        rs_ready, qn_ready, cos_ready = Count(core, "qk_rs"), Count(core, "qk_qn"), Count(core, "qk_cos")
        sin_ready, out_ready = Count(core, "qk_sin"), Count(core, "qk_out")
        rope_in, ba_in, ba_hi, ba_lo = core.sem("rope_in"), core.sem("ba_in"), core.sem("ba_hi"), core.sem("ba_lo")
        kc_done, v_done, v_out = core.sem("kc_done"), core.sem("v_done"), core.sem("v_out")
        ba_done, ba_out = core.sem("ba_done"), core.sem("ba_out")

        def each_tile(eng, body):
            for j in range(2):
                body(j, 0, j, "first")
            with eng.Fori(1, NT // 2 - 1) as i:
                for j in range(2):
                    body(i * 2 + j, i, j, "")
            for j in range(2):
                body(NT - 2 + j, NT // 2 - 1, j, "last")

        with nc.Block() as block:
            @block.sync
            def _(sp):
                for j in range(2):
                    w.load(sp, j, d["w_qk_at"][:, j], j, first=True)
                sp.dma_start(rope[:, :, :], d["rope"]).then_inc(rope_in, 16)
                sp.dma_start(w_ba[:, :, :], d["w_ba"]).then_inc(ba_in, 16)
                with sp.Fori(1, NT // 2) as i:
                    for j in range(2):
                        w.load(sp, i * 2 + j, d["w_qk_at"][:, bass.ds(i * 2 + j, 1)].rearrange("p a k m -> p (a k) m"), j)
                for j in range(2):
                    w.load(sp, NT + j, d["w_v_at"][:, j], j)

            @block.gpsimd
            def _(pool):
                cos_ready.open(pool)
                pool.wait_ge(ba_in, 16)
                pool.tensor_copy(w_ba_hi[:, :, :], w_ba[:, :, :]).then_inc(ba_hi, 1)
                pool.wait_ge(ba_hi, 1)
                pool.tensor_tensor(w_ba_lo[:, :, :], w_ba[:, :, :], w_ba_hi[:, :, :].bitcast(F32),
                                   ALU.subtract).then_inc(ba_lo, 1)
                for j in range(2):
                    w.split_tile(pool, j, 0, j)
                pool.wait_ge(rope_in, 16)

                def tile(t, half, j, place):
                    if place != "last":
                        w.split_tile(pool, t + 2, half + 1, j)
                    qn_ready.wait(pool, t + 1)
                    sin_ready.wait(pool, t)
                    out_ready.wait(pool, t)
                    pool.tensor_tensor(by_cos[:, :], qn[:, :], rope[:, 0, :], ALU.mult).then_inc(cos_ready.sem, 1)
                each_tile(pool, tile)
                pool.wait_ge(kc_done, 1)
                for j in range(2):
                    w.split_tile(pool, NT + j, NT // 2, j, freed=False)

            @block.tensor
            def _(pe):
                w.used.open(pe)
                ss_done.open(pe), rot_done.open(pe)
                pe.wait_ge(w.split, 1)
                for b in range(2):
                    mm = w.product(pe, ps_main[0][:, b * HALF:(b + 1) * HALF], 0, core.h_hi, core.h_lo, b * HALF, HALF)
                mm.then_inc(w.used.sem, 1)

                def rotate(t):
                    qn_ready.wait(pe, t + 1)
                    sin_ready.wait(pe, t)
                    for c in range(2):
                        mm = pe.matmul(ps_rot[:, c * HALF:(c + 1) * HALF], mats[:, C_ROT, :],
                                       qn[:, c * HALF:(c + 1) * HALF], start=True, stop=True)
                    mm.then_inc(rot_done.sem, 1)

                def tile(t, half, j, place):
                    more = not (place == "last" and j == 1)
                    for b in range(2):
                        o = slice(b * HALF, (b + 1) * HALF)
                        if more:
                            if b == 0:
                                pe.wait_ge(w.split, t + 2)
                                raw_ready.wait(pe, t)
                            mm = w.product(pe, ps_main[1 - j][:, o], 1 - j, core.h_hi, core.h_lo, b * HALF, HALF)
                            if b == 1:
                                mm.then_inc(w.used.sem, 1)
                        if b == 0 and not (place == "first" and j == 0):
                            rotate(t - 1)
                        if b == 0:
                            sq_ready.wait(pe, t + 1)
                            std_ready.wait(pe, t)
                            for c in range(2):
                                mm = pe.matmul(ps_ss[:, c * HALF:(c + 1) * HALF], mats[:, C_ONE, :],
                                               sq[:, c * HALF:(c + 1) * HALF], start=True, stop=True)
                            mm.then_inc(ss_done.sem, 1)
                each_tile(pe, tile)
                std_ready.wait(pe, NT)
                raw_ready.wait(pe, NT)
                for g in range(KV_HEADS):
                    mm = w.product(pe, ps_main[0][:, g * CTX:(g + 1) * CTX], g, core.h_hi, core.h_lo, SEQ, CTX)
                mm.then_inc(kc_done, 1)
                rotate(NT - 1)
                pe.wait_ge(ba_lo, 1)
                for c in range(NCH):
                    tk = slice(c * P, (c + 1) * P)
                    for k in range(KT):
                        o = ps_main[1][:, c * 32:(c + 1) * 32]
                        pe.matmul(o, core.h_hi[:, k, tk], w_ba_hi[:, k, :], start=(k == 0), stop=False)
                        pe.matmul(o, core.h_hi[:, k, tk], w_ba_lo[:, k, :], start=False, stop=False)
                        mm = pe.matmul(o, core.h_lo[:, k, tk], w_ba_hi[:, k, :], start=False, stop=(k == KT - 1))
                mm.then_inc(ba_done, 1)
                pe.wait_ge(sq_ready.sem, NT + 1 + sq_ready.slack)
                pe.matmul(ps_ss[:, 0:2 * CTX], mats[:, C_ONE, :], sq[:, 0:2 * CTX], start=True,
                          stop=True).then_inc(ss_done.sem, 1)
                pe.wait_ge(w.split, NT + 2)
                sin_ready.wait(pe, NT)
                for c in range(NCH):
                    tk = slice(c * P, (c + 1) * P)
                    if c >= 2:
                        pe.wait_ge(v_out, c - 1)
                    o = ps_rot[:, (c % 2) * HALF:(c % 2) * HALF + KV_HEADS * P].rearrange("p (g n) -> p g n", g=KV_HEADS)
                    for k in range(KT):
                        pe.matmul(o, core.h_hi[:, k, tk], w.hi2[:, :, k, :], start=(k == 0), stop=False)
                        pe.matmul(o, core.h_hi[:, k, tk], w.lo2[:, :, k, :], start=False, stop=False)
                        mm = pe.matmul(o, core.h_lo[:, k, tk], w.hi2[:, :, k, :], start=False, stop=(k == KT - 1))
                    mm.then_inc(v_done, 1)

            @block.scalar
            def _(act):
                sq_ready.open(act), raw_ready.open(act), std_ready.open(act)

                def tile(t, half, j, place):
                    w.used.wait(act, t + 1)
                    act.activation(sq[:, :], ps_main[j][:, :], ACT.Square).then_inc(sq_ready.sem, 1)
                    qn_ready.wait(act, t)
                    act.activation(raw[:, :], ps_main[j][:, :], ACT.Copy,
                                   scale=a.qk_norm[:, bass.ds(t, 1)]).then_inc(raw_ready.sem, 1)
                    ss_done.wait(act, t + 1)
                    rs_ready.wait(act, t)
                    act.activation(std[:, :], ps_ss[:, :], ACT.Sqrt, scale=1.0 / P,
                                   bias=core.eps[:, 0:1]).then_inc(std_ready.sem, 1)
                each_tile(act, tile)
                n = 2 * CTX
                act.wait_ge(kc_done, 1)
                act.activation(sq[:, 0:n], ps_main[0][:, 0:n], ACT.Square).then_inc(sq_ready.sem, 1)
                qn_ready.wait(act, NT)
                act.activation(raw[:, 0:n], ps_main[0][:, 0:n], ACT.Copy,
                               scale=a.qk_norm[:, NT - 1:NT]).then_inc(raw_ready.sem, 1)
                ss_done.wait(act, NT + 1)
                rs_ready.wait(act, NT)
                act.activation(std[:, 0:n], ps_ss[:, 0:n], ACT.Sqrt, scale=1.0 / P,
                               bias=core.eps[:, 0:1]).then_inc(std_ready.sem, 1)
                act.wait_ge(ba_done, 1)
                act.activation(core.ba[:, :, :], ps_main[1][:, 0:NCH * 32].rearrange("p (c n) -> p c n", n=32),
                               ACT.Copy).then_inc(ba_out, 1)
                for c in range(NCH):
                    act.wait_ge(v_done, c + 1)
                    act.activation(a.v_tok[:, c, :], ps_rot[:, (c % 2) * HALF:(c % 2) * HALF + 256],
                                   ACT.Copy).then_inc(v_out, 1)

            @block.vector
            def _(dve):
                rs_ready.open(dve), qn_ready.open(dve), sin_ready.open(dve), out_ready.open(dve)
                dve.wait_ge(rope_in, 16)

                def tile(t, half, j, place):
                    std_ready.wait(dve, t + 1)
                    out_ready.wait(dve, t)
                    dve.reciprocal(rs[:, :], std[:, :]).then_inc(rs_ready.sem, 1)
                    rs_ready.wait(dve, t + 1)
                    raw_ready.wait(dve, t + 1)
                    cos_ready.wait(dve, t)
                    rot_done.wait(dve, t)
                    dve.tensor_tensor(qn[:, :], raw[:, :], rs[:, :], ALU.mult).then_inc(qn_ready.sem, 1)
                    rot_done.wait(dve, t + 1)
                    o = a.qk[:, bass.ds(t, 1), :].rearrange("p a n -> p (a n)")
                    dve.tensor_tensor(rs[:, :], ps_rot[:, :], rope[:, 1, :], ALU.mult).then_inc(sin_ready.sem, 1)
                    sin_ready.wait(dve, t + 1)
                    cos_ready.wait(dve, t + 1)
                    dve.tensor_tensor(o, rs[:, :], by_cos[:, :], ALU.add).then_inc(out_ready.sem, 1)
                each_tile(dve, tile)
                n = 2 * CTX
                std_ready.wait(dve, NT + 1)
                out_ready.wait(dve, NT)
                dve.reciprocal(rs[:, 0:n], std[:, 0:n]).then_inc(rs_ready.sem, 1)
                rs_ready.wait(dve, NT + 1)
                raw_ready.wait(dve, NT + 1)
                dve.tensor_tensor(a.k_ctx[:, :], raw[:, 0:n], rs[:, 0:n], ALU.mult).then_inc(qn_ready.sem, 1)


def window_attention(core, d, a):
    nc, vec, mats = core.nc, core.vec, core.mats
    SC = float(P) ** -0.5
    W0 = 512
    ROUND = 2 * XCH
    with ExitStack() as st:
        qs = core.sb("q_staged", [P, 2, SEQ], ctx=st)
        sinks = core.sb("sink_staged", [P, 2, 2], ctx=st)
        neg_sink = core.sb("neg_sink", [P, HEADS], ctx=st)
        prob = core.sb("probs", [P, 2, W0 + CTX], ctx=st)
        prob_t = core.sb("probs_t", [P, 2, W0 + CTX], ctx=st)
        o_tok = core.sb("o_tok", [P, 2, P], ctx=st)
        y = core.sb("y_attn", [P, 2, SEQ], ctx=st)
        stat = core.sb("softmax_stats", [P, 2, 8], ctx=st)
        w_ada = [core.sb(f"late_w_ada{j}", [P, KT, SLOT_T * P], ctx=st) for j in range(2)]
        late = core.sb("late_modulation", [P, 4 * KT], ctx=st)
        MODS = 2 * SLOT_T
        assert MODS * (HEADS // 2) == 4 * KT
        ada_in = [core.sem(f"late_ada_in{j}") for j in range(2)]
        mod_made = core.sem("late_mod_made")
        ps_s = [core.ps(f"ps_scores{j}", [P, 1024], ctx=st) for j in range(2)]
        ps_t = core.ps("ps_probs_t", [P, 1024], ctx=st)
        ps_o = core.ps("ps_o", [P, HALF], ctx=st)
        ps_y = core.ps("ps_y", [P, HALF], ctx=st)
        neg_ready, turns = core.sem("neg_sink_ready"), core.sem("stage_turns")
        staged = Count(core, "q_staged_ready")
        scored, transposed = Count(core, "scored"), Count(core, "probs_transposed")
        weighted, turned = Count(core, "pv_done"), Count(core, "o_turned")
        mx_ready, nm_ready, mx_sum = Count(core, "mx_ready"), Count(core, "nm_ready"), Count(core, "denominators")
        exp_ready, sink_ready = Count(core, "exp_ready"), Count(core, "sink_exp_ready")
        rinv_ready, o_ready = Count(core, "rinv_ready"), Count(core, "o_ready")
        pt_act, pt_dve, y_ready = Count(core, "pt_act"), Count(core, "pt_dve"), Count(core, "y_ready")
        y_stored = [core.sem(f"y_stored{j}") for j in range(2)]

        def window(b):
            return list(range(max(0, b - 1), min(XCH, b + 2)))

        def rounds(eng, body):
            for g in range(KV_HEADS):
                with eng.Fori(0, GROUPS // 2) as i:
                    body(g, i + g * (GROUPS // 2))

        with nc.Block() as block:
            @block.gpsimd
            def _(pool):
                staged.open(pool)
                pool.tensor_scalar(neg_sink[:, :], vec[:, V_SINK:V_SINK + HEADS], -1.0, 0.0, ALU.mult,
                                   ALU.add).then_inc(neg_ready, 1)
                pool.wait_ge(neg_ready, 1)

                def body(g, r):
                    for jj in range(2):
                        scored.wait(pool, r * ROUND)
                        rinv_ready.wait(pool, r * ROUND)
                        pool.sem_inc(turns, 1)
                        h = r * 2 + jj
                        pool.tensor_copy(qs[:, jj, :], a.qk[:, bass.ds(h, 1), :].rearrange("p a n -> p (a n)"))
                        pool.tensor_copy(sinks[:, jj, 0:1], vec[:, bass.ds(V_SINK + h, 1)])
                        pool.tensor_copy(sinks[:, jj, 1:2], neg_sink[:, bass.ds(h, 1)]).then_inc(staged.sem, 1)
                rounds(pool, body)

            @block.tensor
            def _(pe):
                scored.open(pe), transposed.open(pe), weighted.open(pe), turned.open(pe)

                def body(g, r):
                    n0 = r * ROUND

                    def scores(u):
                        jj, b = u // XCH, u % XCH
                        if b == 0:
                            staged.wait(pe, r * 2 + jj + 1)
                        exp_ready.wait(pe, n0 + u - 1)
                        ps, q = ps_s[u % 2], qs[:, jj, b * P:(b + 1) * P]
                        win = window(b)
                        c0 = W0 - len(win) * P
                        if win[0] == b - 1:
                            pe.matmul(ps[:, c0:c0 + P], core.id_b[:, :], core.neg_b[:, 0, :], start=True,
                                      stop=False, skip_group_check=True)
                        if win[-1] == b + 1:
                            pe.matmul(ps[:, W0 - P:W0], core.id_b[:, :], core.neg_b[:, 1, :], start=(b == 0),
                                      stop=False, skip_group_check=True)
                        pe.matmul(ps[:, c0:W0], q, a.qk[:, HEADS + g, win[0] * P:(win[-1] + 1) * P],
                                  start=False, stop=True, skip_group_check=True)
                        pe.matmul(ps[:, W0:W0 + CTX], q, a.k_ctx[:, g * CTX:(g + 1) * CTX],
                                  start=True, stop=True).then_inc(scored.sem, 1)

                    def turn_probs(u):
                        exp_ready.wait(pe, n0 + u + 1)
                        pt_act.wait(pe, n0 + u)
                        pt_dve.wait(pe, n0 + u)
                        c0 = W0 - len(window(u % XCH)) * P
                        for c in range(c0, W0 + CTX, P):
                            mm = pe.transpose(ps_t[:, c:c + P], prob[:, u % 2, c:c + P], mats[:, C_ID, :])
                        mm.then_inc(transposed.sem, 1)

                    def values(u):
                        pt_act.wait(pe, n0 + u + 1)
                        pt_dve.wait(pe, n0 + u + 1)
                        o_ready.wait(pe, n0 + u)
                        blocks = window(u % XCH) + list(range(XCH, NCH))
                        c0 = W0 - len(window(u % XCH)) * P
                        for n, kb in enumerate(blocks):
                            mm = pe.matmul(ps_o[:, 0:P], prob_t[:, u % 2, c0 + n * P:c0 + (n + 1) * P],
                                           a.v_tok[:, kb, g * P:(g + 1) * P], start=(n == 0),
                                           stop=(n == len(blocks) - 1))
                        mm.then_inc(weighted.sem, 1)

                    def turn_out(u):
                        o_ready.wait(pe, n0 + u + 1)
                        y_ready.wait(pe, n0 + u)
                        n = u - (ROUND - MODS)
                        if n >= 0:
                            j, m = n // SLOT_T, n % SLOT_T
                            if m == 0:
                                pe.wait_ge(ada_in[j], r * 16 + 16)
                            for k in range(KT):
                                pe.matmul(ps_y[:, P + n:P + n + 1], w_ada[j][:, k, m * P:(m + 1) * P],
                                          core.silu_c[:, k, 0:1], start=(k == 0), stop=(k == KT - 1))
                        pe.transpose(ps_y[:, 0:P], o_tok[:, u % 2, :], mats[:, C_ID, :]).then_inc(turned.sem, 1)

                    for s in range(-1, ROUND + 2):
                        if 0 <= s + 1 < ROUND:
                            scores(s + 1)
                        if 0 <= s < ROUND:
                            turn_probs(s)
                        if 0 <= s - 1 < ROUND:
                            values(s - 1)
                        if 0 <= s - 2 < ROUND:
                            turn_out(s - 2)
                rounds(pe, body)

            @block.scalar
            def _(act):
                act.sem_inc(y_stored[0], 16), act.sem_inc(y_stored[1], 16)
                exp_ready.open(act), sink_ready.open(act), pt_act.open(act), y_ready.open(act)

                def body(g, r):
                    n0 = r * ROUND

                    def probs(u):
                        jj, b = u // XCH, u % XCH
                        c0 = W0 - len(window(b)) * P
                        nm_ready.wait(act, n0 + u + 1)
                        transposed.wait(act, n0 + u - 1)
                        rinv_ready.wait(act, n0 + u - 1)
                        act.activation(prob[:, u % 2, c0:W0 + CTX], ps_s[u % 2][:, c0:W0 + CTX], ACT.Exp, scale=SC,
                                       bias=stat[:, u % 2, 1:2], accum_out=stat[:, u % 2, 2:3]).then_inc(exp_ready.sem, 1)
                        act.activation(stat[:, u % 2, 3:4], sinks[:, jj, 0:1], ACT.Exp,
                                       bias=stat[:, u % 2, 1:2]).then_inc(sink_ready.sem, 1)

                    def evacuate(u):
                        transposed.wait(act, n0 + u + 1)
                        weighted.wait(act, n0 + u - 1)
                        act.activation(prob_t[:, u % 2, W0:W0 + CTX], ps_t[:, W0:W0 + CTX], ACT.Copy).then_inc(pt_act.sem, 1)

                    def result(u):
                        jj, b = u // XCH, u % XCH
                        turned.wait(act, n0 + u + 1)
                        if b == 0:
                            act.wait_ge(y_stored[jj], r * 16 + 16)
                        if u == ROUND - 1:
                            act.activation(late[:, bass.ds(r * MODS, MODS)], ps_y[:, P:P + MODS], ACT.Copy)
                        act.activation(y[:, jj, b * P:(b + 1) * P], ps_y[:, 0:P], ACT.Copy).then_inc(y_ready.sem, 1)

                    for s in range(ROUND + 2):
                        if s < ROUND:
                            probs(s)
                        if s < ROUND:
                            evacuate(s)
                        if 0 <= s - 2 < ROUND:
                            result(s - 2)
                rounds(act, body)

            @block.vector
            def _(dve):
                mx_ready.open(dve), nm_ready.open(dve), rinv_ready.open(dve), pt_dve.open(dve), o_ready.open(dve)
                dve.wait_ge(neg_ready, 1)

                def body(g, r):
                    n0 = r * ROUND

                    def maximum(u):
                        jj, b = u // XCH, u % XCH
                        c0 = W0 - len(window(b)) * P
                        scored.wait(dve, n0 + u + 1)
                        if b == 0:
                            staged.wait(dve, r * 2 + jj + 1)
                        exp_ready.wait(dve, n0 + u - 1)
                        sink_ready.wait(dve, n0 + u - 1)
                        dve.tensor_reduce(stat[:, u % 2, 0:1], ps_s[u % 2][:, c0:W0 + CTX], AX.X,
                                          ALU.max).then_inc(mx_ready.sem, 1)
                        mx_ready.wait(dve, n0 + u + 1)
                        dve.tensor_scalar(stat[:, u % 2, 1:2], stat[:, u % 2, 0:1], -SC, sinks[:, jj, 1:2], ALU.mult,
                                          ALU.min).then_inc(nm_ready.sem, 1)

                    def evacuate(u):
                        c0 = W0 - len(window(u % XCH)) * P
                        transposed.wait(dve, n0 + u + 1)
                        weighted.wait(dve, n0 + u - 1)
                        dve.tensor_copy(prob_t[:, u % 2, c0:W0], ps_t[:, c0:W0]).then_inc(pt_dve.sem, 1)

                    def scale(u):
                        weighted.wait(dve, n0 + u + 1)
                        turned.wait(dve, n0 + u - 1)
                        dve.tensor_scalar(o_tok[:, u % 2, :], ps_o[:, 0:P], stat[:, u % 2, 5:6], None,
                                          ALU.mult).then_inc(o_ready.sem, 1)

                    def denominator(u):
                        sink_ready.wait(dve, n0 + u + 1)
                        exp_ready.wait(dve, n0 + u + 1)
                        dve.tensor_tensor(stat[:, u % 2, 4:5], stat[:, u % 2, 2:3], stat[:, u % 2, 3:4],
                                          ALU.add).then_inc(mx_sum.sem, 1)
                        mx_sum.wait(dve, n0 + u + 1)
                        dve.reciprocal(stat[:, u % 2, 5:6], stat[:, u % 2, 4:5]).then_inc(rinv_ready.sem, 1)

                    for s in range(-1, ROUND + 1):
                        if 0 <= s + 1 < ROUND:
                            maximum(s + 1)
                        if 0 <= s - 1 < ROUND:
                            scale(s - 1)
                        if 0 <= s < ROUND:
                            denominator(s)
                            evacuate(s)
                mx_sum.open(dve)
                rounds(dve, body)
                y_ready.wait(dve, HEADS * XCH)
                dve.tensor_tensor(core.mod[:, 2 * KT:6 * KT, 0], late[:, :], vec[:, V_BADA + 2 * KT:V_BADA + 6 * KT],
                                  ALU.add).then_inc(mod_made, 1)
                dve.wait_ge(mod_made, 1)
                dve.scalar_tensor_tensor(out=core.scale_ffn[:, :], in0=core.mod[:, 4 * KT:5 * KT, 0], scalar=1.0,
                                         in1=vec[:, V_NFFN:V_NFFN + KT], op0=ALU.add, op1=ALU.mult)
                dve.tensor_copy(core.gate_mix[:, :], core.mod[:, 2 * KT:3 * KT, 0])
                dve.tensor_copy(core.gate_ffn[:, :], core.mod[:, 5 * KT:6 * KT, 0])

            @block.sync
            def _(sp):
                def body(g, r):
                    for j in range(2):
                        y_ready.wait(sp, r * ROUND)
                        n = r * 2 + j + 2 * KT // SLOT_T
                        sp.dma_start(w_ada[j][:, :, :], d["w_ada"][:, bass.ds(n, 1)].rearrange(
                            "p a k m -> p (a k) m")).then_inc(ada_in[j], 16)
                    for jj in range(2):
                        y_ready.wait(sp, r * ROUND + (jj + 1) * XCH)
                        sp.dma_start(core.y_dram[:, bass.ds(r * 2 + jj, 1), :].rearrange("p a n -> p (a n)"),
                                     y[:, jj, :]).then_inc(y_stored[jj], 16)
                rounds(sp, body)
                for jj in range(2):
                    sp.wait_ge(y_stored[jj], HEADS // 2 * 16 + 16)


def merge_branch(core, st, w, y_hi, y_lo, y_parts, tag, w_dram, store, add=None):
    nc = core.nc
    sig = core.sb(f"{tag}_sig", [P, 2, SEQ], ctx=st)
    mrg = core.sb(f"{tag}_merged", [P, 2, SEQ], ctx=st)
    prev = core.sb(f"{tag}_prev", [P, 2, SEQ], ctx=st) if add is not None else None
    ps_g = [core.ps(f"{tag}_ps_gate{j}", [P, SEQ], ctx=st) for j in range(2)]
    ps_b = [core.ps(f"{tag}_ps_branch{j}", [P, SEQ], ctx=st) for j in range(2)]
    sig_ready, mrg_ready, add_ready = Count(core, f"{tag}_sig_ready"), Count(core, f"{tag}_mrg"), Count(core, f"{tag}_add")
    stored = [core.sem(f"{tag}_stored{j}") for j in range(2)]
    prev_in = [core.sem(f"{tag}_prev_in{j}") for j in range(2)]
    final = add_ready if add is not None else mrg_ready
    s_sync, s_scalar, s_vector, y_split = y_parts

    def tile_of(dram, t):
        return dram[:, bass.ds(t, 1), :].rearrange("p a n -> p (a n)")

    def sync(sp):
        for j in range(2):
            w.load(sp, j, w_dram[:, j], j, first=True)
        s_sync(sp)
        if add is not None:
            for j in range(2):
                sp.dma_start(prev[:, j, :], add[:, j, :]).then_inc(prev_in[j], 16)
        with sp.Fori(0, KT // 2 - 1) as i:
            steps(sp, i, True)
        steps(sp, KT // 2 - 1, False)
        for j in range(2):
            sp.wait_ge(stored[j], KT // 2 * 16 + 16)

    def steps(sp, i, more):
        for j in range(2):
            m = i * 2 + j
            for s in range(2):
                if more or j == 0:
                    t = m * 2 + s + 2
                    w.load(sp, t, w_dram[:, bass.ds(t, 1)].rearrange("p a k m -> p (a k) m"), s)
            final.wait(sp, m + 1)
            sp.dma_start(tile_of(store, m), mrg[:, j, :]).then_inc(stored[j], 16)
            if add is not None and more:
                sp.dma_start(prev[:, j, :], tile_of(add, m + 2)).then_inc(prev_in[j], 16)

    def pool(p):
        with p.Fori(0, KT) as m:
            for s in range(2):
                w.split_tile(p, m * 2 + s, m, s)

    def tensor(pe):
        w.used.open(pe)

        def step(m, j, first):
            pe.wait_ge(w.split, m * 2 + 1)
            sig_ready.wait(pe, m - 1)
            for b in range(2):
                mm = w.product(pe, ps_g[j][:, b * HALF:(b + 1) * HALF], 0, core.h_hi, core.h_lo, b * HALF, HALF)
            mm.then_inc(w.used.sem, 1)
            pe.wait_ge(w.split, m * 2 + 2)
            mrg_ready.wait(pe, m - 1)
            for b in range(2):
                mm = w.product(pe, ps_b[j][:, b * HALF:(b + 1) * HALF], 1, y_hi, y_lo, b * HALF, HALF,
                               parts=y_split if first and b == 0 else None)
            mm.then_inc(w.used.sem, 1)
        for j in range(2):
            step(j, j, j == 0)
        with pe.Fori(1, KT // 2) as i:
            for j in range(2):
                step(i * 2 + j, j, False)

    def scalar(act):
        sig_ready.open(act)
        s_scalar(act)
        with act.Fori(0, KT // 2) as i:
            for j in range(2):
                m = i * 2 + j
                w.used.wait(act, m * 2 + 1)
                mrg_ready.wait(act, m - 1)
                act.activation(sig[:, j, :], ps_g[j][:, :], ACT.Sigmoid).then_inc(sig_ready.sem, 1)

    def vector(dve):
        mrg_ready.open(dve), add_ready.open(dve)
        dve.sem_inc(stored[0], 16), dve.sem_inc(stored[1], 16)
        s_vector(dve)
        with dve.Fori(0, KT // 2) as i:
            for j in range(2):
                m = i * 2 + j
                sig_ready.wait(dve, m + 1)
                w.used.wait(dve, m * 2 + 2)
                dve.wait_ge(stored[j], i * 16 + 16)
                dve.tensor_tensor(mrg[:, j, :], ps_b[j][:, :], sig[:, j, :], ALU.mult).then_inc(mrg_ready.sem, 1)
                if add is not None:
                    mrg_ready.wait(dve, m + 1)
                    dve.wait_ge(prev_in[j], i * 16 + 16)
                    dve.tensor_tensor(mrg[:, j, :], mrg[:, j, :], prev[:, j, :], ALU.add).then_inc(add_ready.sem, 1)

    return sync, pool, tensor, scalar, vector


def split_from_dram(core, st, tag, src, hi, lo):
    full = core.sb(f"{tag}_full", [P, 2, SEQ], ctx=st)
    full_in = [core.sem(f"{tag}_full_in{j}") for j in range(2)]
    hi_ready, lo_ready = core.sem(f"{tag}_hi_ready"), core.sem(f"{tag}_lo_ready")

    def sync(sp):
        for k in range(KT):
            if k >= 2:
                sp.wait_ge(lo_ready, k - 1)
            sp.dma_start(full[:, k % 2, :], src[:, k, :]).then_inc(full_in[k % 2], 16)

    def scalar(act):
        for k in range(KT):
            act.wait_ge(full_in[k % 2], 16 * (k // 2 + 1))
            act.activation(hi[:, k, :], full[:, k % 2, :], ACT.Copy).then_inc(hi_ready, 1)

    def vector(dve):
        for k in range(KT):
            dve.wait_ge(full_in[k % 2], 16 * (k // 2 + 1))
            dve.wait_ge(hi_ready, k + 1)
            dve.tensor_tensor(lo[:, k, :], full[:, k % 2, :], hi[:, k, :].bitcast(F32), ALU.subtract).then_inc(lo_ready, 1)

    return sync, scalar, vector, lo_ready


def merge_stage(core, tag, y_src, w_dram, store, add=None):
    with ExitStack() as st:
        w = Weights(core, st, tag)
        y_hi = core.sb(f"{tag}_y_hi", [P, KT, SEQ], F32R, ctx=st)
        y_lo = core.sb(f"{tag}_y_lo", [P, KT, SEQ], F32R, ctx=st)
        y_parts = split_from_dram(core, st, tag, y_src, y_hi, y_lo)
        sync, pool, tensor, scalar, vector = merge_branch(core, st, w, y_hi, y_lo, y_parts, tag, w_dram, store, add)
        with core.nc.Block() as block:
            block.sync(sync)
            block.gpsimd(pool)
            block.tensor(tensor)
            block.scalar(scalar)
            block.vector(vector)


class Attention:
    pass


def attention(core, d):
    a = Attention()
    with ExitStack() as st:
        a.qk_norm = core.vec[:, V_QKN:V_QKN + HEADS + KV_HEADS]
        a.qk = core.sb("qk_heads", [P, HEADS + KV_HEADS, SEQ], ctx=st)
        a.k_ctx = core.sb("k_ctx", [P, KV_HEADS * CTX], ctx=st)
        a.v_tok = core.sb("v_tok", [P, NCH, KV_HEADS * P], ctx=st)
        attention_projections(core, d, a)
        window_attention(core, d, a)
    merge_stage(core, "at", core.y_dram, d["w_mg_at"], core.merged_dram)


K_G, K_BETA, K_EG, K_NEG_EG, K_BETA_REST, K_TOTAL = range(6)
NK = 6


def decays(core, d, per_head):
    nc, vec, mats = core.nc, core.vec, core.mats
    SERIES = 8
    with ExitStack() as st:
        def t3(name):
            return core.sb(name, [P, NCH, 2 * HEADS], ctx=st)
        xa, m, e, z, z2, poly, g, beta = (t3(f"decay_{n}") for n in ("xa", "m", "e", "z", "z2", "poly", "g", "beta"))
        ex = core.sb("decay_exps", [P, NCH, 3, 2 * HEADS], ctx=st)
        a_exp = core.sb("a_exp", [P, 2 * HEADS], ctx=st)
        ps = core.ps("ps_sums", [P, NCH, 3, 2 * HEADS], ctx=st)
        v, s, sums, out = core.sem("decay_dve"), core.sem("decay_act"), core.sem("decay_pe"), core.sem("decay_out")
        row = lambda col: vec[:, col:col + 2 * HEADS].unsqueeze(1).broadcast_to([P, NCH, 2 * HEADS])
        nv = [0]

        with nc.Block() as block:
            @block.vector
            def _(dve):
                def chain(ins):
                    nv[0] += 1
                    ins.then_inc(v, 1)
                    dve.wait_ge(v, nv[0])
                a_in = core.ba[:, :, 2 * HEADS:]
                chain(dve.tensor_tensor(xa[:, :, :], a_in, row(V_DT), ALU.add))
                chain(dve.tensor_scalar(z[:, :, :], xa[:, :, :], -1.0, None, ALU.mult))
                chain(dve.tensor_tensor(m[:, :, :], xa[:, :, :], z[:, :, :], ALU.min))
                dve.wait_ge(s, 1)
                chain(dve.tensor_scalar(z[:, :, :], e[:, :, :], 2.0, None, ALU.add))
                chain(dve.reciprocal(z[:, :, :], z[:, :, :]))
                chain(dve.tensor_tensor(z[:, :, :], z[:, :, :], e[:, :, :], ALU.mult))
                chain(dve.tensor_tensor(z2[:, :, :], z[:, :, :], z[:, :, :], ALU.mult))
                chain(dve.tensor_scalar(poly[:, :, :], z2[:, :, :], 1.0 / (2 * SERIES + 1), None, ALU.mult))
                for n in range(SERIES - 1, 0, -1):
                    chain(dve.scalar_tensor_tensor(out=poly[:, :, :], in0=poly[:, :, :], scalar=1.0 / (2 * n + 1),
                                                   in1=z2[:, :, :], op0=ALU.add, op1=ALU.mult))
                chain(dve.scalar_tensor_tensor(out=poly[:, :, :], in0=poly[:, :, :], scalar=1.0, in1=z[:, :, :],
                                               op0=ALU.add, op1=ALU.mult))
                chain(dve.tensor_scalar(m[:, :, :], xa[:, :, :], 0.0, None, ALU.max))
                chain(dve.scalar_tensor_tensor(out=m[:, :, :], in0=poly[:, :, :], scalar=2.0, in1=m[:, :, :],
                                               op0=ALU.mult, op1=ALU.add))
                dve.wait_ge(s, 2)
                ab = a_exp[:, :].unsqueeze(1).broadcast_to([P, NCH, 2 * HEADS])
                chain(dve.tensor_tensor(m[:, :, :], m[:, :, :], ab, ALU.mult))
                dve.tensor_scalar(g[:, :, :], m[:, :, :], -1.0, None, ALU.mult).then_inc(v, 1)
                nv[0] += 1
                dve.wait_ge(v, nv[0])
                dve.wait_ge(s, 4)
                chain(dve.tensor_tensor(ex[:, :, 1, :], ex[:, :, 1, :], beta[:, :, :], ALU.mult))
                chain(dve.tensor_scalar(m[:, :, :], ex[:, :, 0, :], -1.0, None, ALU.mult))
                for kind, src in ((K_G, g[:, :, :]), (K_BETA, beta[:, :, :]), (K_EG, ex[:, :, 0, :]),
                                  (K_NEG_EG, m[:, :, :]), (K_BETA_REST, ex[:, :, 1, :]), (K_TOTAL, ex[:, :, 2, :])):
                    for di in range(2):
                        dve.tensor_copy(per_head[:, :, kind, :, di].rearrange("p h c -> p c h"),
                                        src[:, :, di * HEADS:(di + 1) * HEADS]).then_inc(out, 1)
                dve.wait_ge(out, 2 * NK)

            @block.scalar
            def _(act):
                act.wait_ge(v, 3)
                act.activation(e[:, :, :], m[:, :, :], ACT.Exp).then_inc(s, 1)
                act.activation(a_exp[:, :], vec[:, V_ALOG:V_ALOG + 2 * HEADS], ACT.Exp).then_inc(s, 1)
                act.activation(beta[:, :, :], core.ba[:, :, 0:2 * HEADS], ACT.Sigmoid).then_inc(s, 1)
                act.wait_ge(sums, 1)
                act.activation(ex[:, :, :, :], ps[:, :, :, :], ACT.Exp).then_inc(s, 1)

            @block.tensor
            def _(pe):
                pe.wait_ge(v, 8 + (SERIES - 1) + 5)
                for c in range(NCH):
                    for di, (incl, rest) in enumerate(((C_GE, C_LT), (C_LE, C_GT))):
                        h = slice(di * HEADS, (di + 1) * HEADS)
                        pe.matmul(ps[:, c, 0, h], mats[:, incl, :], g[:, c, h], start=True, stop=True)
                        pe.matmul(ps[:, c, 1, h], mats[:, rest, :], g[:, c, h], start=True, stop=True)
                    mm = pe.matmul(ps[:, c, 2, :], mats[:, C_ONE, :], g[:, c, :], start=True, stop=True)
                mm.then_inc(sums, 1)


PADW = SEQ + CTX + 8
CVW = SEQ + CTX + 4
CTX0 = SEQ + 4
T_K, T_V, T_Q, T_GATE = range(4)
PROJ = [(T_K, 0), (T_K, 1), (T_K, 2), (T_V, 0), (T_V, 1), (T_V, 2), (T_Q, 0), (T_Q, 1), (T_GATE, 0), (T_GATE, 1)]
TILE_END = {T_K: 3, T_V: 6, T_Q: 8, T_GATE: 10}
NPROJ = len(PROJ)
SPREAD = [(0, 4), (4, 4), (XCH, NCH - XCH)]
BT = NCH // 2
MERGES = LEVELS - 1
E_SCALE = 2048.0
ORDER = [list(range(XCH, NCH)) + list(range(XCH)), list(range(NCH - 1, XCH - 1, -1)) + list(range(XCH - 1, -1, -1))]


def at_chunk(c):
    return c * CH if c < XCH else CTX0 + (c - XCH) * CH


def delta_net(core, d):
    nc, vec, mats = core.nc, core.vec, core.mats
    with ExitStack() as st:
        per_head = core.sb("per_head_columns", [P, HEADS, NK, NCH, 2], ctx=st)
        decays(core, d, per_head)
        sb = lambda name, shape, dt=F32: core.sb(name, shape, dt, ctx=st)
        ring, tile_bytes = nc.sbuf_base, KT * P * 4
        sb("ring_region", [P, 6 * KT * P])
        w = Weights(core, st, "dn", at=ring)
        id_e = sb("identity_e_scale", [P, P])
        col = sb("head_columns", [P, NK, NCH, 2])
        taps = sb("head_taps", [P, 3, TAPS])
        gl = sb("g_masked", [P, 2, 4, P])
        dec = sb("decay_t", [P, 2, 2, P])
        bf = sb("b_full", [P, NCH, 2, P])
        qkd = sb("qk_decayed_t", [P, XCH, 2, P])
        q_t, k_t = sb("q_t", [P, SEQ]), sb("k_t", [P, CVW])
        kv_tok = sb("kv_tok", [P, 2 * NCH, P])
        state = sb("state", [P, 2, 2, P])
        rv = sb("r_and_v", [P, 2, 3, P])
        gate = sb("gate_silu", [P, SEQ])
        o_acc = sb("o_acc", [P, XCH, P])
        o_norm = sb("o_normed", [P, XCH, P])
        o_stat = sb("o_stats", [P, 3, XCH])
        k_stat = sb("k_stats", [P, 2, NCH])
        q_stat = sb("q_stats", [P, XCH])
        up = lambda n: (n + 31) // 32 * 32
        cv_bytes, pad_bytes, line = up(3 * CVW * 4), up(2 * PADW * 4), up(CVW * 4)
        base = nc.sbuf_base
        sb("shared_region", [P, (cv_bytes + pad_bytes + 2 * line) // 4 + 8])
        place = lambda name, shape, at, dt=F32: nc.alloc_sbuf_tensor_at(name, shape, dt, offset=base + at)
        cv = place("conv_out", [P, 3, CVW], 0)
        pad = place("conv_in", [P, 2, PADW], cv_bytes)
        sq = place("dn_squares", [P, CVW], cv_bytes + pad_bytes)
        diag = place("k_rstd_diagonals", [P, NCH, P], cv_bytes + pad_bytes + line)
        size = NCH * 2 * P * 2
        x_h, y_h = place("x_half", [P, NCH, 2, P], 0, F16), place("y_half", [P, NCH, 2, P], size, F16)
        pm = place("p_masked", [P, 2, 4, P], 2 * size, F16)
        e_h = place("residual_half", [P, 2, 4, P], 2 * size + 2048, F16)
        b_h = place("b_half", [P, NCH, 2, P], cv_bytes, F16)
        x_f = place("x_full", [P, NCH, 2, P], cv_bytes + size, F32)
        y_full = [nc.alloc_sbuf_tensor_at(f"y_full{j}", [P, 2, 4 * P], F32, offset=ring + slot * tile_bytes)
                  for j, slot in enumerate((Weights.HI + 1, Weights.LO + 1))]
        y_f = [y_full[0][:, 0, :], y_full[0][:, 1, :], y_full[1][:, 0, :], y_full[1][:, 1, :],
               o_norm[:, 0:4, :].rearrange("p m n -> p (m n)")]
        assert 2 * size + 4096 <= cv_bytes and size * 3 <= pad_bytes + 2 * line
        bank = [core.ps(f"dn_bank{b}", [P, HALF], ctx=st) for b in range(8)]

        def slots(t, bt):
            return t[:, 2 * bt:2 * bt + 2, :, :]

        def flat(t, bt):
            return slots(t, bt).rearrange("p c d n -> p (c d n)")

        C = lambda name: Count(core, f"dn_{name}")
        grp, ssd, tr, dps, kqd = C("grp"), C("ssd"), C("tr"), C("dps"), C("kqd")
        bcd = C("k_rstd_spread")
        pd, xyp, rd_, y2d = C("p_done"), C("xy_done"), C("res_done"), C("y2_done")
        ksd, xrd, oqd, otd = C("ks_done"), C("xr_done"), C("oq_done"), C("o_turned")
        evac, sil, sqd, stdc = C("evac"), C("silu"), C("squares"), C("std")
        tka, kqc, dct, bhd = C("tok_act"), C("kq_copied"), C("decay"), C("b_rounded")
        xyd, osq = C("xy_copied"), C("o_std")
        qsd, ovr = C("q_sums_copied"), C("o_var")
        cvs, rec, nrm, tkd, bqd = C("conv_steps"), C("rec"), C("normed"), C("tok_dve"), C("b_made")
        x1d, pmd, yhd = C("x_first"), C("p_masked_made"), C("y_rounded")
        ed, yfd = C("residual"), C("inverse_made")
        rdy, vd, stt, o1, od = C("r_made"), C("v_made"), C("state_made"), C("o_first"), C("o_added")
        orec, onr, fin = C("o_rec"), C("o_normed_made"), C("y_made")
        colc, tapc, padz, bfd, oz = C("columns"), C("taps"), C("pad_zeroed"), C("b_with_i"), C("o_zeroed")
        gld, y1d, dgd = C("g_masked"), C("y_first"), C("k_rstd_diag")
        ystored, turns = core.sem("dn_y_stored"), core.sem("dn_pool_turns")
        id_made = core.sem("dn_identity_made")

        def heads(eng, prologue, body):
            prologue()
            with eng.Fori(0, HEADS - 1) as h:
                body(h, True)
            body(HEADS - 1, False)

        def pe_group(pe, hn, s, part):
            tile, r = PROJ[s]
            t0, n = RANGES[r]
            j = tile % 2
            if part == 0:
                pe.wait_ge(w.split, hn * 4 + tile + 1)
                evac.wait(pe, hn * NPROJ + (s - 2 if s >= 3 else 0))
            mms = [(k, v) for k in range(KT) for v in range(3)]
            for k, v in mms[part * KT:(part + 1) * KT]:
                wt = w.lo[j] if v == 2 else w.hi[j]
                x = core.h_lo if v == 1 else core.h_hi
                mm = pe.matmul(bank[4 + s % 3][:, 0:n], wt[:, k, :], x[:, k, t0:t0 + n], start=(k == 0 and v == 0),
                               stop=(k == KT - 1 and v == 2))
            if part == 2:
                mm.then_inc(grp.sem, 1)

        def pe_sum(pe, hn, tile):
            chunks, n = (XCH, 2) if tile == T_Q else (NCH, 1)
            sqd.wait(pe, hn * 2 + n)
            nrm.wait(pe, hn * 3 + (3 if tile == T_Q else 0))
            qsd.wait(pe, hn)
            for c in range(chunks):
                mm = pe.matmul(bank[7][:, c:c + 1], sq[:, at_chunk(c):at_chunk(c) + CH], mats[:, C_ONE, 0:1], start=True,
                               stop=True)
            mm.then_inc(ssd.sem, 1)

        def pe_spread(pe, hn, r):
            if r == 0:
                dgd.wait(pe, hn + 1)
                stdc.wait(pe, hn + 1)
            if r == 1:
                evac.wait(pe, hn * NPROJ + 8)
            if r == 2:
                nrm.wait(pe, hn * 3 + 1)
            c0, n = SPREAD[r]
            pe.matmul(bank[(7, 5)[r % 2]][:, 0:n * P], mats[:, C_ONE, :],
                      diag[:, c0:c0 + n, :].rearrange("p c n -> p (c n)"), start=True, stop=True).then_inc(bcd.sem, 1)

        def pe_prepare(pe, h):
            fin.wait(pe, h * 2)
            qsd.wait(pe, h + 1)
            evac.wait(pe, h * NPROJ + NPROJ)
            for g in range(5):
                if g == 0:
                    nrm.wait(pe, h * 3 + 3)
                if g == 2:
                    sil.wait(pe, h * 3 + 2)
                for n in range(4):
                    c = 4 * g + n
                    src = cv[:, c // NCH, at_chunk(c % NCH):at_chunk(c % NCH) + CH]
                    mm = pe.transpose(bank[(0, 1, 2, 3, 7)[g]][:, n * P:(n + 1) * P], src, mats[:, C_ID, :])
                mm.then_inc(tr.sem, 1)
            sil.wait(pe, h * 3 + 3)
            for bt in range(BT):
                gld.wait(pe, h * 5 + bt + 1)
                dct.wait(pe, h * 5 + bt - 1)
                for n in range(4):
                    o, di = bank[4 + bt % 2][:, n * P:(n + 1) * P], n % 2
                    pe.matmul(o, core.id_b[:, :], core.neg_b[:, di, :], start=True, stop=False)
                    mm = pe.matmul(o, gl[:, bt % 2, n, :], mats[:, (C_GE, C_LE)[di], :], start=False, stop=True)
                mm.then_inc(dps.sem, 1)
                bqd.wait(pe, h * 5 + bt)
                for n in range(2):
                    c = 2 * bt + n
                    k = cv[:, 0, at_chunk(c):at_chunk(c) + CH]
                    mm = pe.matmul(bank[6][:, n * P:(n + 1) * P], k, k, start=True, stop=True)
                    if c < XCH:
                        mm = pe.matmul(bank[6][:, (2 + n) * P:(3 + n) * P], k, cv[:, 2, c * CH:(c + 1) * CH],
                                       start=True, stop=True)
                mm.then_inc(kqd.sem, 1)

        def pe_inverse(pe, h):
            tka.wait(pe, h * 3 + 3)
            tkd.wait(pe, h * 2 + 2)
            bqd.wait(pe, h * 5 + 5)
            N = MERGES * BT

            def p(n):
                lv, bt = divmod(n, BT)
                x1d.wait(pe, h * 5 + min(n - 1, 5))
                pmd.wait(pe, h * N + n - BT - 1)
                if lv == 0:
                    bhd.wait(pe, h * 5 + bt + 1)
                elif lv > 1:
                    xyd.wait(pe, h * N + n - 2 * BT + 1)
                for m in range(4):
                    c, di = 2 * bt + m // 2, m % 2
                    x = x_h[:, c, di, :] if lv else core.id_h[:, :]
                    mm = pe.matmul(bank[n % 2][:, m * P:(m + 1) * P], b_h[:, c, di, :], x, start=True, stop=True)
                mm.then_inc(pd.sem, 1)

            def xy(n):
                bt = n % BT
                pmd.wait(pe, h * N + n + 1)
                xyd.wait(pe, h * N + n - 1)
                if n < BT:
                    y1d.wait(pe, h * 5 + bt + 1)
                bx, by = bank[2 + n % 2], bank[6 + n % 2]
                pe.matmul(bx[:, :], core.id_h[:, :], flat(x_h, bt), start=True, stop=False)
                for m in range(4):
                    pe.matmul(bx[:, m * P:(m + 1) * P], y_h[:, 2 * bt + m // 2, m % 2, :], pm[:, n % 2, m, :],
                              start=False, stop=(m == 3))
                pe.matmul(by[:, :], core.id_h[:, :], flat(y_h, bt), start=True, stop=False)
                for m in range(4):
                    mm = pe.matmul(by[:, m * P:(m + 1) * P], pm[:, n % 2, m, :], y_h[:, 2 * bt + m // 2, m % 2, :],
                                   start=False, stop=(m == 3))
                mm.then_inc(xyp.sem, 1)
            for n in range(BT + N + 1):
                if n < BT + N:
                    p(n)
                if n >= BT + 1:
                    xy(n - BT - 1)
            dct.wait(pe, h * 5 + 5)
            for bt in range(BT + 1):
                if bt < BT:
                    xyd.wait(pe, h * N + N - BT + bt + 1)
                    ed.wait(pe, h * 5 + bt - 1)
                    for m in range(4):
                        c, di = 2 * bt + m // 2, m % 2
                        mm = pe.matmul(bank[4 + bt % 2][:, m * P:(m + 1) * P], bf[:, c, di, :],
                                       x_f[:, c, di, :], start=True, stop=True)
                    mm.then_inc(rd_.sem, 1)
                if bt >= 1:
                    b = bt - 1
                    ed.wait(pe, h * 5 + b + 1)
                    yhd.wait(pe, h * 5 + b + 1)
                    yfd.wait(pe, h * 5 + b - 1)
                    pmd.wait(pe, h * N + N)
                    for m in range(4):
                        c, di = 2 * b + m // 2, m % 2
                        mm = pe.matmul(bank[b % 2][:, m * P:(m + 1) * P], e_h[:, b % 2, m, :], y_h[:, c, di, :],
                                       start=True, stop=True)
                    mm.then_inc(y2d.sem, 1)

        def pe_chain(pe, h, fill):
            yfd.wait(pe, h * 5 + 5)
            xyd.wait(pe, h * MERGES * BT + MERGES * BT)
            kqc.wait(pe, h + 1)
            for s in range(NCH):
                cs = [ORDER[di][s] for di in range(2)]
                for di in range(2):
                    stt.wait(pe, h * 20 + 2 * s + di + 1)
                    pe.matmul(bank[di][:, 0:P], k_t[:, at_chunk(cs[di]):at_chunk(cs[di]) + CH], state[:, di, s % 2, :],
                              start=True, stop=True).then_inc(ksd.sem, 1)
                if fill:
                    pe_group(pe, h + 1, s, 0)
                for di in range(2):
                    rdy.wait(pe, h * 20 + 2 * s + di + 1)
                    pe.matmul(bank[di][:, 0:P], bf[:, cs[di], di, :], rv[:, di, 0, :], start=True,
                              stop=True).then_inc(xrd.sem, 1)
                if fill:
                    pe_group(pe, h + 1, s, 1)
                for di in range(2):
                    c = cs[di]
                    vd.wait(pe, h * 20 + 2 * s + di + 1)
                    if s >= 3:
                        od.wait(pe, h * 16 + 2 * (s - 3) + di + 1)
                    if s < NCH - 1:
                        mm = pe.matmul(bank[2 + di][:, 2 * P:3 * P], kv_tok[:, c, :], rv[:, di, 1, :], start=True,
                                       stop=True)
                    if c < XCH:
                        pe.matmul(bank[2 + di][:, 0:P], q_t[:, c * CH:(c + 1) * CH], state[:, di, s % 2, :],
                                  start=True, stop=True)
                        mm = pe.matmul(bank[2 + di][:, P:2 * P], qkd[:, c, di, :], rv[:, di, 2, :], start=True,
                                       stop=True)
                    mm.then_inc(oqd.sem, 1)
                if fill:
                    pe_group(pe, h + 1, s, 2)
                    if s == 7:
                        pe_sum(pe, h + 1, T_K)
                    if s == 9:
                        pe_spread(pe, h + 1, 0)
                        pe_spread(pe, h + 1, 1)
            if fill:
                pe_spread(pe, h + 1, 2)
            vd.wait(pe, h * 20 + 20)
            onr.wait(pe, h + 1)
            for b in range(2):
                for n in range(4):
                    mm = pe.transpose(bank[b][:, n * P:(n + 1) * P], o_norm[:, 4 * b + n, :], mats[:, C_ID, :])
                mm.then_inc(otd.sem, 1)
            if fill:
                pe_sum(pe, h + 1, T_Q)

        def tensor(pe):
            for c in (grp, ssd, bcd, tr, dps, kqd, pd, xyp, rd_, y2d, ksd, xrd, oqd, otd):
                c.open(pe)

            def prologue():
                for s in range(NPROJ):
                    for part in range(3):
                        pe_group(pe, 0, s, part)
                    if s == 7:
                        pe_sum(pe, 0, T_K)
                for r in range(3):
                    pe_spread(pe, 0, r)
                pe_sum(pe, 0, T_Q)

            def body(h, fill):
                pe_prepare(pe, h)
                pe_inverse(pe, h)
                pe_chain(pe, h, fill)
            heads(pe, prologue, body)

        def act_evacuate(act, hn, s):
            tile, r = PROJ[s]
            t0, n = RANGES[r]
            grp.wait(act, hn * NPROJ + s + 1)
            if tile == T_GATE:
                fin.wait(act, hn * 2)
                act.activation(gate[:, t0:t0 + n], bank[4 + s % 3][:, 0:n], ACT.Silu).then_inc(evac.sem, 1)
                return
            if r == 0:
                cvs.wait(act, hn * 15 + (5 if tile == T_Q else 0))
                yfd.wait(act, hn * 5)
            at = 2 + t0 + (4 if r == 2 else 0)
            act.activation(pad[:, 1 if tile == T_V else 0, at:at + n], bank[4 + s % 3][:, 0:n],
                           ACT.Copy).then_inc(evac.sem, 1)

        def act_silu(act, hn, tile):
            n = SEQ if tile == T_Q else CVW
            cvs.wait(act, hn * 15 + 5 * tile + 5)
            act.activation(cv[:, tile, 0:n], cv[:, tile, 0:n], ACT.Silu).then_inc(sil.sem, 1)

        def act_square(act, hn, tile):
            n = SEQ if tile == T_Q else CVW
            sil.wait(act, hn * 3 + tile + 1)
            ssd.wait(act, hn * 2 + (1 if tile == T_Q else 0))
            act.activation(sq[:, 0:n], cv[:, tile, 0:n], ACT.Square).then_inc(sqd.sem, 1)

        def act_std(act, hn):
            ssd.wait(act, hn * 2 + 1)
            rec.wait(act, hn)
            act.activation(k_stat[:, 0, :], bank[7][:, 0:NCH], ACT.Sqrt, bias=core.eps[:, 0:1]).then_inc(stdc.sem, 1)

        def act_step(act, hn, s):
            if 1 <= s < 9:
                act_evacuate(act, hn, s - 1)
            if s == 6:
                act_silu(act, hn, T_K)
                act_square(act, hn, T_K)
            if s == 8:
                act_std(act, hn)
            if s == 9:
                act_silu(act, hn, T_V)

        def act_tail_q(act, hn):
            act_silu(act, hn, T_Q)
            act_square(act, hn, T_Q)

        def act_gates(act, hn):
            for s in (8, 9):
                act_evacuate(act, hn, s)

        def act_body(act, h, fill):
            for g in (0, 2, 4):
                tr.wait(act, h * 5 + g + 1)
                act.activation(kv_tok[:, 4 * g:4 * g + 4, :].rearrange("p c n -> p (c n)"),
                               bank[(0, 1, 2, 3, 7)[g]][:, :], ACT.Copy).then_inc(tka.sem, 1)

            nrm.wait(act, h * 3 + 3)
            sil.wait(act, h * 3 + 3)
            act.activation(q_t[:, :], cv[:, T_Q, 0:SEQ], ACT.Copy)
            act.activation(k_t[:, :], cv[:, T_K, :], ACT.Copy).then_inc(kqc.sem, 1)
            for bt in range(BT + 1):
                if bt < BT:
                    dps.wait(act, h * 5 + bt + 1)
                    bqd.wait(act, h * 5 + bt)
                    act.activation(dec[:, :, :, :].rearrange("p c d n -> p (c d n)"), bank[4 + bt % 2][:, :],
                                   ACT.Exp).then_inc(dct.sem, 1)
                if bt >= 1:
                    bfd.wait(act, h * 5 + bt)
                    act.activation(flat(b_h, bt - 1), flat(bf, bt - 1), ACT.Copy).then_inc(bhd.sem, 1)
            for n in range(MERGES * BT):
                last = n >= (MERGES - 1) * BT
                xyp.wait(act, h * MERGES * BT + n + 1)
                act.activation(flat(x_f if last else x_h, n % BT), bank[2 + n % 2][:, :], ACT.Copy)
                act.activation(y_f[n % BT] if last else flat(y_h, n % BT), bank[6 + n % 2][:, :],
                               ACT.Copy).then_inc(xyd.sem, 1)
            if fill:
                for s in range(NCH):
                    act_step(act, h + 1, s)
            od.wait(act, h * 16 + 16)
            otd.wait(act, h * 2)
            for c in range(XCH):
                ins = act.activation(o_norm[:, c, :], o_acc[:, c, :], ACT.Square, accum_out=o_stat[:, 0, c:c + 1])
            ins.then_inc(osq.sem, 1)
            ovr.wait(act, h + 1)
            act.activation(o_stat[:, 2, :], o_stat[:, 1, :], ACT.Sqrt).then_inc(osq.sem, 1)
            if fill:
                act_tail_q(act, h + 1)
                act_gates(act, h + 1)

        def scalar(act):
            for c in (evac, sil, sqd, stdc, tka, kqc, dct, bhd, xyd, osq):
                c.open(act)

            def prologue():
                for s in range(NCH):
                    act_step(act, 0, s)
                act_tail_q(act, 0)
                act_gates(act, 0)
            heads(act, prologue, lambda h, fill: act_body(act, h, fill))

        def dve_conv(dve, hn, tile, js):
            n = SEQ if tile == T_Q else CVW
            src, dst = pad[:, 1 if tile == T_V else 0, :], cv[:, tile, 0:n]
            for j in js:
                if j == 0:
                    evac.wait(dve, hn * NPROJ + TILE_END[tile])
                    padz.wait(dve, hn + 1)
                    tapc.wait(dve, hn + 1)
                    yfd.wait(dve, hn * 5)
                    ins = dve.tensor_scalar(dst, src[:, 0:n], taps[:, tile_at(tile), 0:1], None, ALU.mult)
                else:
                    cvs.wait(dve, hn * 15 + tile * 5 + j)
                    ins = dve.scalar_tensor_tensor(out=dst, in0=src[:, j:j + n], scalar=taps[:, tile_at(tile), j:j + 1],
                                                   in1=dst, op0=ALU.mult, op1=ALU.add)
                ins.then_inc(cvs.sem, 1)

        def tile_at(tile):
            return {T_Q: 0, T_K: 1, T_V: 2}[tile]

        def dve_step(dve, hn, s, part):
            taps_of = {4: (T_K, (0, 1, 2)), 5: (T_K, (3, 4)), 7: (T_V, (0, 1, 2)), 8: (T_V, (3, 4)), 9: (T_Q, (0, 1, 2))}
            tile, js = taps_of.get(s, (T_K, ()))
            dve_conv(dve, hn, tile, js[part:part + 1])
            if s == 8 and part == 0:
                dve_root(dve, hn)
            if s == 9 and part == 2:
                dve_norm(dve, hn, 0)

        def dve_root(dve, hn):
            stdc.wait(dve, hn + 1)
            dgd.wait(dve, hn)
            dve.reciprocal(k_stat[:, 1, :], k_stat[:, 0, :]).then_inc(rec.sem, 1)

        def dve_q_sums(dve, hn):
            ssd.wait(dve, hn * 2 + 2)
            ovr.wait(dve, hn)
            dve.tensor_scalar(q_stat[:, :], bank[7][:, 0:XCH], P * EPS, P * EPS * EPS, ALU.mult,
                              ALU.add).then_inc(qsd.sem, 1)

        def dve_norm(dve, hn, r):
            c0, n = SPREAD[r]
            bcd.wait(dve, hn * 3 + r + 1)
            sqd.wait(dve, hn * 2 + 1)
            at = at_chunk(c0)
            dve.tensor_tensor(cv[:, T_K, at:at + n * P], cv[:, T_K, at:at + n * P], bank[(7, 5)[r % 2]][:, 0:n * P],
                              ALU.mult).then_inc(nrm.sem, 1)

        def dve_chain(dve, h, fill):
            for di in range(2):
                dve.memset(state[:, di, 0, :], 0.0).then_inc(stt.sem, 1)
            for s in range(NCH):
                cs = [ORDER[di][s] for di in range(2)]
                cnt = [h * 20 + 2 * s + di + 1 for di in range(2)]
                for di in range(2):
                    ksd.wait(dve, cnt[di])
                    dve.scalar_tensor_tensor(out=rv[:, di, 0, :], in0=bank[di][:, 0:P],
                                             scalar=col[:, K_NEG_EG, cs[di], di:di + 1], in1=kv_tok[:, NCH + cs[di], :],
                                             op0=ALU.mult, op1=ALU.add).then_inc(rdy.sem, 1)
                if fill:
                    dve_step(dve, h + 1, s, 0)
                for di in range(2):
                    xrd.wait(dve, cnt[di])
                    dve.tensor_scalar(rv[:, di, 1, :], bank[di][:, 0:P], col[:, K_BETA_REST, cs[di], di:di + 1], None,
                                      ALU.mult)
                    dve.tensor_scalar(rv[:, di, 2, :], bank[di][:, 0:P], col[:, K_BETA, cs[di], di:di + 1], None,
                                      ALU.mult).then_inc(vd.sem, 1)
                if fill:
                    dve_step(dve, h + 1, s, 1)
                for di in range(2):
                    c = cs[di]
                    oqd.wait(dve, cnt[di])
                    if s < NCH - 1:
                        dve.scalar_tensor_tensor(out=state[:, di, (s + 1) % 2, :], in0=state[:, di, s % 2, :],
                                                 scalar=col[:, K_TOTAL, c, di:di + 1], in1=bank[2 + di][:, 2 * P:3 * P],
                                                 op0=ALU.mult, op1=ALU.add).then_inc(stt.sem, 1)
                for di in range(2):
                    c = cs[di]
                    if c < XCH:
                        n = h * 16 + 2 * (s - 2)
                        oz.wait(dve, h + 1)
                        od.wait(dve, n)
                        dve.scalar_tensor_tensor(out=o_acc[:, c, :], in0=bank[2 + di][:, 0:P],
                                                 scalar=col[:, K_EG, c, di:di + 1], in1=o_acc[:, c, :], op0=ALU.mult,
                                                 op1=ALU.add).then_inc(o1.sem, 1)
                for di in range(2):
                    c = cs[di]
                    if c < XCH:
                        o1.wait(dve, h * 16 + 2 * (s - 2) + di + 1)
                        dve.tensor_tensor(o_acc[:, c, :], o_acc[:, c, :], bank[2 + di][:, P:2 * P],
                                          ALU.add).then_inc(od.sem, 1)
                if fill:
                    dve_step(dve, h + 1, s, 2)

        def dve_body(dve, h, fill):
            for g in (1, 3):
                tr.wait(dve, h * 5 + g + 1)
                dve.tensor_copy(kv_tok[:, 4 * g:4 * g + 4, :].rearrange("p c n -> p (c n)"),
                                bank[(0, 1, 2, 3, 7)[g]][:, :]).then_inc(tkd.sem, 1)
            colc.wait(dve, h + 1)
            for bt in range(BT):
                kqd.wait(dve, h * 5 + bt + 1)
                dct.wait(dve, h * 5 + bt + 1)
                if bt < XCH // 2:
                    qk = bank[6][:, 2 * P:4 * P].rearrange("p (c n) -> p c n", c=2).unsqueeze(2).broadcast_to([P, 2, 2, P])
                    dve.tensor_tensor(slots(qkd, bt), qk, dec[:, :, :, :], ALU.mult)
                for n in range(4):
                    c, di = 2 * bt + n // 2, n % 2
                    ins = dve.scalar_tensor_tensor(out=bf[:, c, di, :], in0=bank[6][:, (n // 2) * P:(n // 2 + 1) * P],
                                                   scalar=col[:, K_BETA, c, di:di + 1], in1=dec[:, n // 2, di, :],
                                                   op0=ALU.mult, op1=ALU.mult)
                ins.then_inc(bqd.sem, 1)
            N = MERGES * BT
            kqc.wait(dve, h + 1)
            for n in range(BT + N):
                m = C_LEVEL + 2 * (n // BT)
                mask = mats[:, m:m + 2, :].rearrange("p d n -> p (d n)").unsqueeze(1).broadcast_to([P, 2, 2 * P])
                pd.wait(dve, h * (BT + N) + n + 1)
                p = bank[n % 2][:, :].rearrange("p (c n) -> p c n", c=2)
                if n < BT:
                    dve.tensor_tensor(slots(x_h, n).rearrange("p c d n -> p c (d n)"), p, mask,
                                      ALU.mult).then_inc(x1d.sem, 1)
                    continue
                xyp.wait(dve, h * N + n - BT - 1)
                dve.tensor_tensor(pm[:, (n - BT) % 2, :, :].rearrange("p (c d) n -> p c (d n)", c=2), p, mask,
                                  ALU.mult).then_inc(pmd.sem, 1)
            for bt in range(BT + 1):
                if bt < BT:
                    xyd.wait(dve, h * N + N - BT + bt + 1)
                    dve.tensor_copy(flat(y_h, bt), y_f[bt]).then_inc(yhd.sem, 1)
                    dve.wait_ge(id_made, 1)
                    rd_.wait(dve, h * 5 + bt + 1)
                    y2d.wait(dve, h * 5 + bt - 1)
                    dve.scalar_tensor_tensor(out=e_h[:, bt % 2, :, :],
                                             in0=bank[4 + bt % 2][:, :].rearrange("p (m n) -> p m n", m=4),
                                             scalar=-E_SCALE, in1=id_e[:, :].unsqueeze(1).broadcast_to([P, 4, P]),
                                             op0=ALU.mult, op1=ALU.add).then_inc(ed.sem, 1)
                if bt >= 1:
                    b = bt - 1
                    y2d.wait(dve, h * 5 + b + 1)
                    dve.scalar_tensor_tensor(out=flat(bf, b), in0=bank[b % 2][:, :], scalar=1.0 / E_SCALE, in1=y_f[b],
                                             op0=ALU.mult, op1=ALU.add).then_inc(yfd.sem, 1)
            dve_chain(dve, h, fill)
            if fill:
                dve_norm(dve, h + 1, 1)
                dve_norm(dve, h + 1, 2)
                dve_conv(dve, h + 1, T_Q, (3,))
            osq.wait(dve, h * 2 + 1)
            qsd.wait(dve, h + 1)
            dve.scalar_tensor_tensor(out=o_stat[:, 1, :], in0=o_stat[:, 0, :], scalar=1.0 / P, in1=q_stat[:, :],
                                     op0=ALU.mult, op1=ALU.add).then_inc(ovr.sem, 1)
            if fill:
                dve_conv(dve, h + 1, T_Q, (4,))
            osq.wait(dve, h * 2 + 2)
            dve.reciprocal(o_stat[:, 0, :], o_stat[:, 2, :]).then_inc(orec.sem, 1)
            orec.wait(dve, h + 1)
            dve.tensor_tensor(o_norm[:, :, :], o_acc[:, :, :], o_stat[:, 0, :].unsqueeze(2).broadcast_to([P, XCH, P]),
                              ALU.mult).then_inc(onr.sem, 1)
            onr.wait(dve, h + 1)
            for b in range(2):
                otd.wait(dve, h * 2 + b + 1)
                evac.wait(dve, h * NPROJ + NPROJ)
                dve.scalar_tensor_tensor(out=o_acc[:, 4 * b:4 * b + 4, :].rearrange("p c n -> p (c n)"),
                                         in0=bank[b][:, :], scalar=vec[:, V_DNNORM:V_DNNORM + 1],
                                         in1=gate[:, b * HALF:(b + 1) * HALF], op0=ALU.mult,
                                         op1=ALU.mult).then_inc(fin.sem, 1)
            if fill:
                dve_q_sums(dve, h + 1)

        def vector(dve):
            for c in (qsd, ovr, cvs, rec, nrm, tkd, bqd, x1d, pmd, yhd, ed, yfd, rdy, vd, stt, o1, od, orec, onr, fin):
                c.open(dve)
            dve.tensor_scalar(id_e[:, :], mats[:, C_ID, :], E_SCALE, None, ALU.mult).then_inc(id_made, 1)

            def prologue():
                for s in range(NCH):
                    for part in range(3):
                        dve_step(dve, 0, s, part)
                dve_norm(dve, 0, 1)
                dve_norm(dve, 0, 2)
                dve_conv(dve, 0, T_Q, (3, 4))
                dve_q_sums(dve, 0)
            heads(dve, prologue, lambda h, fill: dve_body(dve, h, fill))

        def pool_split(pool, hn, tile):
            before = {T_K: -2, T_V: None, T_Q: TILE_END[T_K], T_GATE: TILE_END[T_V]}[tile]
            by = (yfd, hn * 5) if tile == T_V else (grp, hn * NPROJ + before)
            w.split_tile(pool, hn * 4 + tile, hn * 2 + tile // 2, tile % 2, by=by)

        def pool_lines(pool, hn):
            yfd.wait(pool, hn * 5)
            cvs.wait(pool, hn * 15)
            pool.sem_inc(turns, 1)
            for a, b in ((0, 2), (SEQ + 2, SEQ + 6), (PADW - 2, PADW)):
                ins = pool.memset(pad[:, :, a:b], 0.0)
            ins.then_inc(padz.sem, 1)
            pool.tensor_copy(taps[:, :, :].rearrange("p a b -> p (a b)"),
                             vec[:, bass.ds(V_CONVD + hn * (3 * TAPS), 3 * TAPS)]).then_inc(tapc.sem, 1)

        def pool_diag(pool, hn):
            rec.wait(pool, hn + 1)
            bcd.wait(pool, hn * 3)
            pool.sem_inc(turns, 1)
            pool.tensor_tensor(diag[:, :, :], mats[:, C_ID, :].unsqueeze(1).broadcast_to([P, NCH, P]),
                               k_stat[:, 1, :].unsqueeze(2).broadcast_to([P, NCH, P]), ALU.mult).then_inc(dgd.sem, 1)

        def pool_body(pool, h, fill):
            fin.wait(pool, h * 2)
            pool.sem_inc(turns, 1)
            pool.tensor_copy(col[:, :, :, :], per_head[:, bass.ds(h, 1), :, :, :].rearrange(
                "p a k c d -> p (a k) c d")).then_inc(colc.sem, 1)

            def masked_g(bt):
                dps.wait(pool, h * 5 + bt - 1)
                if bt == 0:
                    colc.wait(pool, h + 1)
                pool.sem_inc(turns, 1)
                pool.tensor_tensor(gl[:, bt % 2, :, :].rearrange("p (c d) n -> p c d n", c=2),
                                   mats[:, C_LT:C_LT + 2, :].unsqueeze(1).broadcast_to([P, 2, 2, P]),
                                   col[:, K_G, 2 * bt:2 * bt + 2, :].unsqueeze(3).broadcast_to([P, 2, 2, P]),
                                   ALU.mult).then_inc(gld.sem, 1)

            def first_y(bt):
                bfd.wait(pool, h * 5 + bt + 1)
                kqc.wait(pool, h + 1)
                pool.sem_inc(turns, 1)
                mask = mats[:, C_FIRST_T:C_FIRST_T + 2, :].unsqueeze(1).broadcast_to([P, 2, 2, P])
                pool.tensor_tensor(slots(y_h, bt), slots(bf, bt), mask, ALU.mult).then_inc(y1d.sem, 1)
            for bt in range(2):
                masked_g(bt)
            for bt in range(BT):
                bqd.wait(pool, h * 5 + bt + 1)
                pool.sem_inc(turns, 1)
                pool.affine_select(flat(bf, bt), flat(bf, bt), pattern=[[0, 4], [1, P]], compare_op=ALU.not_equal,
                                   fill=1.0, base=0, channel_multiplier=-1).then_inc(bfd.sem, 1)
                if bt + 2 < BT:
                    masked_g(bt + 2)
            for bt in range(BT):
                first_y(bt)
            pool.wait_ge(ystored, h * 16 + 16)
            pool.sem_inc(turns, 1)
            pool.memset(o_acc[:, :, :], 0.0).then_inc(oz.sem, 1)
            if fill:
                pool_split(pool, h + 1, T_K)
                pool_split(pool, h + 1, T_V)
                pool_lines(pool, h + 1)
                pool_split(pool, h + 1, T_Q)
                pool_split(pool, h + 1, T_GATE)
                pool_diag(pool, h + 1)

        def gpsimd(pool):
            for c in (colc, tapc, padz, bfd, gld, y1d, dgd, oz):
                c.open(pool)
            pool.sem_inc(ystored, 16)

            def prologue():
                pool_split(pool, 0, T_K)
                pool_split(pool, 0, T_V)
                pool_lines(pool, 0)
                pool_split(pool, 0, T_Q)
                pool_split(pool, 0, T_GATE)
                pool_diag(pool, 0)
            heads(pool, prologue, lambda h, fill: pool_body(pool, h, fill))

        def sync(sp):
            def prologue():
                for n in range(4):
                    w.load(sp, n, d["w_dn"][:, n], n % 2, first=n < 2)

            def body(h, fill):
                if fill:
                    for n in range(4):
                        t = (h + 1) * 4 + n
                        w.load(sp, t, d["w_dn"][:, bass.ds(t, 1)].rearrange("p a k m -> p (a k) m"), n % 2)
                fin.wait(sp, h * 2 + 2)
                sp.dma_start(core.y_dram[:, bass.ds(h, 1), :].rearrange("p a n -> p (a n)"),
                             o_acc[:, :, :].rearrange("p c n -> p (c n)")).then_inc(ystored, 16)
            heads(sp, prologue, body)
            sp.wait_ge(ystored, HEADS * 16 + 16)

        with nc.Block() as block:
            block.sync(sync)
            block.gpsimd(gpsimd)
            block.tensor(tensor)
            block.scalar(scalar)
            block.vector(vector)
    merge_stage(core, "dnm", core.y_dram, d["w_mg_dn"], core.merged2_dram, core.merged_dram)


def output_and_norm(core, d, h_hi, h_lo, h_base, m_hi, m_lo, base):
    nc, mats = core.nc, core.mats
    with ExitStack() as outer:
        x1 = core.sb("x1", [P, KT, SEQ], ctx=outer)
        rstd = core.sb("x1_rstd", [P, SEQ], ctx=outer)
        with ExitStack() as st:
            w = Weights(core, st, "wout", at=base + 2 * KT * SEQ * 4)
            x_in = core.sb("x_residual", [P, 2, SEQ], ctx=st)
            ps = [core.ps(f"ps_out{j}", [P, SEQ], ctx=st) for j in range(2)]
            x_loaded = [core.sem(f"x_res_in{j}") for j in range(2)]
            ps_ss = core.ps("ps_x1_ss", [P, SEQ], ctx=st)
            sq = nc.alloc_sbuf_tensor_at("x1_squares", [P, 2, SEQ], F32, offset=h_base)
            sq_made, ss_done = Count(core, "x1_squares_made"), Count(core, "x1_squares_summed")
            std_made, rstd_made = core.sem("x1_std"), core.sem("x1_rstd_made")
            x1_made, x1_stored = Count(core, "x1_made"), core.sem("x1_stored")
            s_sync, s_scalar, s_vector, m_split = split_from_dram(core, st, "wout", core.merged2_dram, m_hi, m_lo)
            with nc.Block() as block:
                @block.sync
                def _(sp):
                    for j in range(2):
                        w.load(sp, j, d["w_out"][:, j], j, first=True)
                        sp.dma_start(x_in[:, j, :], d["xT"][:, j, 0:SEQ]).then_inc(x_loaded[j], 16)
                    s_sync(sp)
                    with sp.Fori(1, KT // 2) as i:
                        for j in range(2):
                            t = i * 2 + j
                            w.load(sp, t, d["w_out"][:, bass.ds(t, 1)].rearrange("p a k m -> p (a k) m"), j)
                            x1_made.wait(sp, t - 1)
                            sp.dma_start(x_in[:, j, :], d["xT"][:, bass.ds(t, 1), 0:SEQ].rearrange(
                                "p a n -> p (a n)")).then_inc(x_loaded[j], 16)
                    x1_made.wait(sp, KT)
                    sp.dma_start(core.x1_dram, x1[:, :, :]).then_inc(x1_stored, 16)
                    sp.wait_ge(x1_stored, 16)

                @block.gpsimd
                def _(pool):
                    with pool.Fori(0, KT // 2) as i:
                        for j in range(2):
                            w.split_tile(pool, i * 2 + j, i, j)

                @block.scalar
                def _(act):
                    sq_made.open(act)
                    s_scalar(act)
                    with act.Fori(0, KT // 2) as i:
                        for j in range(2):
                            t = i * 2 + j
                            x1_made.wait(act, t + 1)
                            ss_done.wait(act, t - 1)
                            act.activation(sq[:, j, :], x1[:, bass.ds(t, 1), :].rearrange("p a n -> p (a n)"),
                                           ACT.Square).then_inc(sq_made.sem, 1)
                    ss_done.wait(act, KT)
                    act.activation(rstd[:, :], ps_ss[:, :], ACT.Sqrt, scale=1.0 / D_MODEL,
                                   bias=core.eps[:, 0:1]).then_inc(std_made, 1)

                @block.tensor
                def _(pe):
                    w.used.open(pe)
                    ss_done.open(pe)

                    def squares(t, j, first=False, last=False):
                        sq_made.wait(pe, t + 1)
                        for b in range(2):
                            o = slice(b * HALF, (b + 1) * HALF)
                            mm = pe.matmul(ps_ss[:, o], mats[:, C_ONE, :], sq[:, j, o], start=first, stop=last,
                                           skip_group_check=True)
                        mm.then_inc(ss_done.sem, 1)

                    def step(t, j, parts=None):
                        pe.wait_ge(w.split, t + 1)
                        x1_made.wait(pe, t - 1)
                        for b in range(2):
                            mm = w.product(pe, ps[j][:, b * HALF:(b + 1) * HALF], j, m_hi, m_lo, b * HALF, HALF,
                                           parts=parts if b == 0 else None)
                        mm.then_inc(w.used.sem, 1)
                    step(0, 0, m_split)
                    step(1, 1)
                    squares(0, 0, first=True)
                    with pe.Fori(1, KT // 2) as i:
                        for j in range(2):
                            step(i * 2 + j, j)
                            squares(i * 2 + j - 1, 1 - j)
                    squares(KT - 1, 1, last=True)

                @block.vector
                def _(dve):
                    x1_made.open(dve)
                    s_vector(dve)
                    with dve.Fori(0, KT // 2) as i:
                        for j in range(2):
                            t = i * 2 + j
                            w.used.wait(dve, t + 1)
                            dve.wait_ge(x_loaded[j], i * 16 + 16)
                            dve.scalar_tensor_tensor(out=x1[:, bass.ds(t, 1), :].rearrange("p a n -> p (a n)"),
                                                     in0=ps[j][:, :], scalar=core.gate_mix[:, bass.ds(t, 1)],
                                                     in1=x_in[:, j, :], op0=ALU.mult,
                                                     op1=ALU.add).then_inc(x1_made.sem, 1)
                    dve.wait_ge(std_made, 1)
                    dve.reciprocal(rstd[:, :], rstd[:, :]).then_inc(rstd_made, 1)
                    dve.wait_ge(rstd_made, 1)

        with ExitStack() as st:
            line = SEQ * 4
            place = lambda name, shape, n: nc.alloc_sbuf_tensor_at(name, shape, F32, offset=base + n * line)
            xn, hf = (place(name, [P, 2, SEQ], 2 * n) for n, name in enumerate(("x1_normed", "h2_full")))
            xn_ready, hi_ready, hf_ready, lo_ready = (core.sem(f"h2_{n}") for n in ("xn", "hi", "hf", "lo"))
            with nc.Block() as block:
                @block.scalar
                def _(act):
                    for k in range(KT):
                        act.wait_ge(xn_ready, k + 1)
                        if k >= 2:
                            act.wait_ge(lo_ready, k - 1)
                        sc, sh = core.scale_ffn[:, k:k + 1], core.mod[:, 3 * KT + k, 0:1]
                        act.activation(h_hi[:, k, :], xn[:, k % 2, :], ACT.Identity, bias=sh,
                                       scale=sc).then_inc(hi_ready, 1)
                        act.activation(hf[:, k % 2, :], xn[:, k % 2, :], ACT.Identity, bias=sh,
                                       scale=sc).then_inc(hf_ready, 1)

                @block.vector
                def _(dve):
                    def low(k):
                        dve.wait_ge(hf_ready, k + 1)
                        dve.tensor_tensor(h_lo[:, k, :], hf[:, k % 2, :], h_hi[:, k, :].bitcast(F32),
                                          ALU.subtract).then_inc(lo_ready, 1)
                    for k in range(KT):
                        if k >= 2:
                            dve.wait_ge(hf_ready, k - 1)
                        dve.tensor_tensor(xn[:, k % 2, :], x1[:, k, :], rstd[:, :], ALU.mult).then_inc(xn_ready, 1)
                        if k >= 1:
                            low(k - 1)
                    low(KT - 1)


def ffn_up(core, d, h_hi, h_lo, act_t):
    nc, vec = core.nc, core.vec
    with ExitStack() as st:
        w = Weights(core, st, "up")
        pad = core.sb("ffn_pad", [P, 2, SEQ + 2], ctx=st)
        u = core.sb("ffn_u", [P, 2, SEQ], ctx=st)
        ps = [[core.ps(f"ps_up{j}_{s}", [P, SEQ], ctx=st) for s in range(2)] for j in range(2)]
        copied, zeroed = Count(core, "up_copied"), core.sem("up_zeroed")
        conv, gated, made = Count(core, "up_conv"), Count(core, "up_silu"), Count(core, "up_made")
        with nc.Block() as block:
            @block.sync
            def _(sp):
                for s in range(2):
                    w.load(sp, s, d["w_up"][:, s], s, first=True)
                with sp.Fori(1, FT) as m:
                    for s in range(2):
                        t = m * 2 + s
                        w.load(sp, t, d["w_up"][:, bass.ds(t, 1)].rearrange("p a k m -> p (a k) m"), s)

            @block.gpsimd
            def _(pool):
                with pool.Fori(0, FT) as m:
                    for s in range(2):
                        w.split_tile(pool, m * 2 + s, m, s)

            @block.tensor
            def _(pe):
                w.used.open(pe)
                with pe.Fori(0, FT // 2) as i:
                    for j in range(2):
                        for s in range(2):
                            t = (i * 2 + j) * 2 + s
                            pe.wait_ge(w.split, t + 1)
                            copied.wait(pe, t - 3)
                            for b in range(2):
                                mm = w.product(pe, ps[j][s][:, b * HALF:(b + 1) * HALF], s, h_hi, h_lo, b * HALF, HALF)
                            mm.then_inc(w.used.sem, 1)

            @block.scalar
            def _(act):
                copied.open(act), gated.open(act)
                act.wait_ge(zeroed, 1)
                with act.Fori(0, FT // 2) as i:
                    for j in range(2):
                        m = i * 2 + j
                        for s in range(2):
                            w.used.wait(act, m * 2 + s + 1)
                            conv.wait(act, m * 6 - 3 * (1 - s))
                            act.activation(pad[:, s, 1:SEQ + 1], ps[j][s][:, :], ACT.Copy).then_inc(copied.sem, 1)
                        conv.wait(act, m * 6 + 3)
                        act.activation(u[:, 0, :], u[:, 0, :], ACT.Silu).then_inc(gated.sem, 1)

            @block.vector
            def _(dve):
                conv.open(dve), made.open(dve)
                dve.memset(pad[:, :, 0:1], 0.0)
                dve.memset(pad[:, :, SEQ + 1:SEQ + 2], 0.0).then_inc(zeroed, 1)
                dve.wait_ge(zeroed, 1)
                with dve.Fori(0, FT // 2) as i:
                    for j in range(2):
                        m = i * 2 + j
                        for s in range(2):
                            tap = lambda n: vec[:, bass.ds((m + s * FT) * FTAPS + V_CONVF + n, 1)]
                            copied.wait(dve, m * 2 + s + 1)
                            made.wait(dve, m)
                            for n in range(FTAPS):
                                src = pad[:, s, n:n + SEQ]
                                if n == 0:
                                    ins = dve.tensor_scalar(u[:, s, :], src, tap(0),
                                                            vec[:, bass.ds(m + s * FT + V_CONVB, 1)], ALU.mult, ALU.add)
                                else:
                                    conv.wait(dve, m * 6 + s * 3 + n)
                                    ins = dve.scalar_tensor_tensor(out=u[:, s, :], in0=src, scalar=tap(n),
                                                                   in1=u[:, s, :], op0=ALU.mult, op1=ALU.add)
                                ins.then_inc(conv.sem, 1)
                        conv.wait(dve, m * 6 + 6)
                        gated.wait(dve, m + 1)
                        out = act_t[:, :, bass.ds(m, 1), :].rearrange("p h a n -> p h (a n)")
                        dve.tensor_tensor(out, u[:, 0, :].rearrange("p (h n) -> p h n", h=2),
                                          u[:, 1, :].rearrange("p (h n) -> p h n", h=2), ALU.mult).then_inc(made.sem, 1)


def ffn_down(core, d, out, act_t, lo_t):
    nc = core.nc
    KP = FT // 2
    with ExitStack() as st:
        w = Weights(core, st, "down", kt=KP)
        hi_t = core.sb("act_hi", [P, FT, HALF], F32R, ctx=st)
        x_in = core.sb("x1_in", [P, 2, HALF], ctx=st)
        y = core.sb("y_out", [P, 2, HALF], ctx=st)
        ps = [core.ps(f"ps_down{j}", [P, HALF], ctx=st) for j in range(2)]
        hi_ready, lo_ready = core.sem("act_hi_ready"), core.sem("act_lo_ready")
        made = Count(core, "y_made_ffn")
        x_loaded = [core.sem(f"x1_in{j}") for j in range(2)]
        stored = [core.sem(f"out_stored{j}") for j in range(2)]

        def tiles(eng, half, body):
            with eng.Fori(0, KT // 2) as i:
                for j in range(2):
                    body(i * 2 + j, i, j)

        with nc.Block() as block:
            @block.sync
            def _(sp):
                for half in range(2):
                    def body(m, i, j):
                        for part in range(2):
                            t = (m + half * KT) * 2 + part
                            sp.wait_ge(w.split, t - 1 + 2)
                            sp.dma_start(w.raw[part][:, :, :], d["w_down"][:, bass.ds(m, 1), part * KP:(part + 1) * KP].rearrange(
                                "p a k m -> p (a k) m")).then_inc(w.loaded[part], 16)
                        made.wait(sp, half * KT + m - 1)
                        sp.dma_start(x_in[:, j, :], core.x1_dram[:, bass.ds(m, 1), half * HALF:(half + 1) * HALF].rearrange(
                            "p a n -> p (a n)")).then_inc(x_loaded[j], 16)
                    tiles(sp, half, body)

            @block.gpsimd
            def _(pool):
                pool.sem_inc(w.split, 2)
                with pool.Fori(0, 2 * KT) as n:
                    for part in range(2):
                        w.split_tile(pool, n * 2 + part, n, part)

            @block.tensor
            def _(pe):
                w.used.open(pe)
                for half in range(2):
                    def body(m, i, j):
                        n = m + half * KT
                        made.wait(pe, n - 1)
                        for part in range(2):
                            pe.wait_ge(w.split, n * 2 + part + 1 + 2)
                            for k in range(KP):
                                kk = part * KP + k
                                if first:
                                    pe.wait_ge(lo_ready, half * FT + kk + 1)
                                hi, lo = hi_t[:, kk, :], lo_t[:, half, kk, :]
                                pe.matmul(ps[j][:, :], w.hi[part][:, k, :], hi, start=(kk == 0), stop=False)
                                pe.matmul(ps[j][:, :], w.hi[part][:, k, :], lo, start=False, stop=False)
                                mm = pe.matmul(ps[j][:, :], w.lo[part][:, k, :], hi, start=False, stop=(kk == FT - 1))
                            mm.then_inc(w.used.sem, 1)
                    first = True
                    for j in range(2):
                        body(j, 0, j)
                        first = False
                    with pe.Fori(1, KT // 2) as i:
                        for j in range(2):
                            body(i * 2 + j, i, j)

            @block.scalar
            def _(act):
                for half in range(2):
                    if half == 1:
                        w.used.wait(act, 2 * KT)
                    for k in range(FT):
                        act.activation(hi_t[:, k, :], act_t[:, half, k, :], ACT.Copy).then_inc(hi_ready, 1)

                    def body(m, i, j):
                        made.wait(act, m + half * KT + 1)
                        act.dma_start(out[:, bass.ds(m, 1), half * HALF:(half + 1) * HALF].rearrange("p a n -> p (a n)"),
                                      y[:, j, :]).then_inc(stored[j], 16)
                    tiles(act, half, body)
                for j in range(2):
                    act.wait_ge(stored[j], KT * 16 + 16)

            @block.vector
            def _(dve):
                made.open(dve)
                for j in range(2):
                    dve.sem_inc(stored[j], 16)
                for half in range(2):
                    for k in range(FT):
                        dve.wait_ge(hi_ready, half * FT + k + 1)
                        dve.tensor_tensor(lo_t[:, half, k, :], act_t[:, half, k, :], hi_t[:, k, :].bitcast(F32),
                                          ALU.subtract).then_inc(lo_ready, 1)

                    def body(m, i, j):
                        n = m + half * KT
                        w.used.wait(dve, n * 2 + 2)
                        dve.wait_ge(x_loaded[j], (i + half * (KT // 2)) * 16 + 16)
                        dve.wait_ge(stored[j], (i + half * (KT // 2)) * 16 + 16)
                        dve.scalar_tensor_tensor(out=y[:, j, :], in0=ps[j][:, :], scalar=core.gate_ffn[:, bass.ds(m, 1)],
                                                 in1=x_in[:, j, :], op0=ALU.mult, op1=ALU.add).then_inc(made.sem, 1)
                    tiles(dve, half, body)


def channel_mixing(core, d, out):
    nc = core.nc
    with ExitStack() as ffn:
        base = nc.sbuf_base
        core.sb("act_region", [P, 2 * FT * HALF], ctx=ffn)
        act_t = nc.alloc_sbuf_tensor_at("act", [P, 2, FT, HALF], F32, offset=base)
        lo_t = nc.alloc_sbuf_tensor_at("act_lo", [P, 2, FT, HALF], F32R, offset=base)
        m_hi = nc.alloc_sbuf_tensor_at("merged_hi", [P, KT, SEQ], F32R, offset=base)
        m_lo = nc.alloc_sbuf_tensor_at("merged_lo", [P, KT, SEQ], F32R, offset=base + KT * SEQ * 4)
        with ExitStack() as st:
            h_base = nc.sbuf_base
            h_hi = core.sb("h2_hi", [P, KT, SEQ], F32R, ctx=st)
            h_lo = core.sb("h2_lo", [P, KT, SEQ], F32R, ctx=st)
            output_and_norm(core, d, h_hi, h_lo, h_base, m_hi, m_lo, base)
            ffn_up(core, d, h_hi, h_lo, act_t)
        ffn_down(core, d, out, act_t, lo_t)


CHANNEL_STAGES = (channel_mixing,)
STAGES = (modulation_and_norm, attention, delta_net, channel_mixing)


def build_program(nc, d, out, stages=STAGES):
    with ExitStack() as ctx:
        core = Core(nc, ctx)
        core.vec = core.sb("vectors", [P, NVEC])
        core.mats = core.sb("constants", [P, NCONST, P])
        core.id_h = core.sb("identity_half", [P, P], F16)
        core.id_b = core.sb("identity_b", [P, P], BF16)
        core.neg_b = core.sb("neg_masks", [P, 2, P], BF16)
        core.eps = core.sb("eps_columns", [P, 2])
        core.mod = core.sb("modulation", [P, 48, 2])
        core.silu_c = core.sb("silu_c", [P, KT, 2])
        core.scale_mix = core.sb("scale_mix", [P, KT, 2])
        core.scale_ffn = core.sb("scale_ffn", [P, KT])
        core.gate_mix = core.sb("gate_mix", [P, KT])
        core.gate_ffn = core.sb("gate_ffn", [P, KT])
        core.x1_dram = nc.dram_tensor("x1_scratch", (P, KT, SEQ), F32, kind="Internal").ap()
        core.ba = core.sb("b_and_a", [P, NCH, 32])
        core.y_dram = nc.dram_tensor("y_scratch", (P, KT, SEQ), F32, kind="Internal").ap()
        core.merged2_dram = nc.dram_tensor("merged2_scratch", (P, KT, SEQ), F32, kind="Internal").ap()
        core.merged_dram = nc.dram_tensor("merged_scratch", (P, KT, SEQ), F32, kind="Internal").ap()
        with ExitStack() as mixing:
            core.h_hi = core.sb("h_hi", [P, KT, TOK], F32R, ctx=mixing)
            core.h_lo = core.sb("h_lo", [P, KT, TOK], F32R, ctx=mixing)
            for stage in stages:
                if stage in CHANNEL_STAGES:
                    break
                stage(core, d)
                core.retire_semaphores()
        for stage in stages:
            if stage in CHANNEL_STAGES:
                stage(core, d, out)
                core.retire_semaphores()


def lay_out(i):
    def cols(a):
        return np.asarray(a).reshape(-1, P).T

    def tiles(w):
        k, m = w.shape
        return np.ascontiguousarray(w.reshape(k // P, P, m // P, P).transpose(1, 2, 0, 3))

    i = {k: np.asarray(v) for k, v in i.items()}
    both = np.stack([i["c"].reshape(KT, P), i["c_ctx"].reshape(KT, P)], 1)
    conv_f = i["ffn_conv"][0].reshape(FTAPS, 2 * FT, P).transpose(2, 1, 0).reshape(P, -1)
    conv_d = i["dn_conv"][0].reshape(TAPS, 3, HEADS, P).transpose(3, 2, 1, 0).reshape(P, -1)
    row = lambda a: np.broadcast_to(np.asarray(a).reshape(1, -1), (P, np.asarray(a).size))
    vec = np.concatenate([
        both.reshape(2 * KT, P).T, cols(i["b_ada"][0]), cols(i["norm_mix"][0]), cols(i["norm_ffn"][0]),
        cols(i["dn_norm"][0]), *[cols(i["q_norm"][0])] * HEADS, *[cols(i["k_norm"][0])] * KV_HEADS,
        cols(i["ffn_conv_b"][0]), conv_f, conv_d, row(i["attn_sink"][0]), row(i["dn_a_log"][0]),
        row(i["dn_dt_bias"][0])], 1)
    mats, rope = constants()
    w_in = i["w_in"][0]
    sl = lambda a, n: tiles(w_in[:, a:a + n])
    tok = np.concatenate([i["x"][0], i["ctx"][0]], 0)
    w_ada = i["w_ada"][0].reshape(KT, P, 12, 4 * P).transpose(1, 2, 0, 3)
    up = tiles(i["ffn_up"][0])
    return {
        "vec": vec, "mats": mats, "rope": rope,
        "xT": tok.T.reshape(KT, P, TOK).transpose(1, 0, 2),
        "w_ada": w_ada,
        "w_qk_at": sl(COL_AQ, 1280), "w_v_at": sl(COL_AV, 256),
        "w_ba": w_in[:, COL_BA:COL_BA + 32].reshape(KT, P, 32).transpose(1, 0, 2),
        "w_dn": np.stack([sl(c, 1024) for c in (COL_K, COL_V, COL_Q, COL_GATE)], 2).reshape(P, 4 * HEADS, KT, P),
        "w_mg_at": np.stack([sl(COL_MG_AT, 1024), tiles(i["w_branch_attn"][0])], 2).reshape(P, 2 * KT, KT, P),
        "w_mg_dn": np.stack([sl(COL_MG_DN, 1024), tiles(i["w_branch_dn"][0])], 2).reshape(P, 2 * KT, KT, P),
        "w_out": tiles(i["w_out"][0]),
        "w_up": np.stack([up[:, :FT], up[:, FT:]], 2).reshape(P, 2 * FT, KT, P),
        "w_down": tiles(i["ffn_down"][0]),
    }


def kernel(**inputs):
    import concourse.bacc as bacc
    from concourse.bass_utils import run_bass_kernel_spmd

    nc = bacc.Bacc("TRN2", target_bir_lowering=False, num_devices=1, dynamic_dma_scratch_size=1024)
    arrays, d = {}, {}
    for name, a in lay_out(inputs).items():
        a = np.ascontiguousarray(a)
        arrays[f"in_{name}"] = a
        d[name] = nc.dram_tensor(f"in_{name}", a.shape, F32, kind="ExternalInput").ap()
    out = nc.dram_tensor("out_tok", (P, KT, SEQ), F32, kind="ExternalOutput").ap()
    build_program(nc, d, out)
    r = run_bass_kernel_spmd(nc, [arrays], core_ids=[0])
    y = r.results[0]["out_tok"]
    return np.ascontiguousarray(y.transpose(2, 1, 0).reshape(1, SEQ, D_MODEL))
```
